# Optimizing a Trainium2 kernel written in Bass

```python
import jax, jax.numpy as jnp
from jax import lax
import numpy as np
import math
import jax
import jax.numpy as jnp

D_MODEL = 1024
BATCH = 1
SEQ = 256
DEPTH = 1

HEAD_DIM = 64
ATTN_HEADS = 8
ATTN_WIDTH = ATTN_HEADS * HEAD_DIM
ROPE_DIM = HEAD_DIM // 4
ROPE_THETA = 500000.0
DILATED_PATTERNS = ((128, 1), (512, 4), (2048, 16))
HG_HEADS = 4
HG_EXPAND = 128
HG_VDIM = 128
HG_KDIM = HG_HEADS * HG_EXPAND
HG_WIDTH = HG_HEADS * HG_VDIM
HG_CHUNK = 64
MIX_WIDTH = ATTN_WIDTH + HG_WIDTH
IN_SIZES = (ATTN_WIDTH, ATTN_WIDTH, ATTN_WIDTH, HG_KDIM, HG_KDIM, HG_WIDTH, HG_WIDTH)
IN_COLS = sum(IN_SIZES)
D_FF = 2816
EPS = 1e-6
NEG_INF = -1e30


def _rms_norm(x, w):
    xf = x.astype(jnp.float32)
    y = xf * lax.rsqrt(jnp.mean(xf * xf, axis=-1, keepdims=True) + EPS)
    return (y * w.astype(jnp.float32)).astype(x.dtype)

def _swiglu(h, w1, w3, w2):
    return (jax.nn.silu(h @ w1) * (h @ w3)) @ w2

def _rope_tables(s):
    inv = ROPE_THETA ** (-jnp.arange(0, ROPE_DIM, 2, dtype=jnp.float32) / ROPE_DIM)
    ang = jnp.arange(s, dtype=jnp.float32)[:, None] * inv[None, :]
    return jnp.cos(ang), jnp.sin(ang)

def _partial_rope(x, cos, sin):
    half = ROPE_DIM // 2
    xf = x.astype(jnp.float32)
    x1, x2, rest = xf[..., :half], xf[..., half:ROPE_DIM], xf[..., ROPE_DIM:]
    c, s_ = cos[None, :, None, :], sin[None, :, None, :]
    out = jnp.concatenate([x1 * c - x2 * s_, x1 * s_ + x2 * c, rest], axis=-1)
    return out.astype(x.dtype)

def _dilated_branch(q, k, v, window, dilation):
    b, s, h, dh = q.shape
    w = window // dilation
    l = s // dilation
    nb = -(-l // w)
    lp = nb * w
    bb = b * dilation

    def to_sub(t):
        t = t.reshape(b, l, dilation, h, dh).transpose(0, 2, 1, 3, 4).reshape(bb, l, h, dh)
        return jnp.pad(t, ((0, 0), (0, lp - l), (0, 0), (0, 0)))

    def windows(t):
        t = jnp.pad(t, ((0, 0), (w, 0), (0, 0), (0, 0))).reshape(bb, nb + 1, w, h, dh)
        return jnp.concatenate([t[:, :-1], t[:, 1:]], axis=2)

    qb = to_sub(q).reshape(bb, nb, w, h, dh)
    kw, vw = windows(to_sub(k)), windows(to_sub(v))
    scores = jnp.einsum('bnqhd,bnkhd->bnhqk', qb, kw,
                        preferred_element_type=jnp.float32) * (dh ** -0.5)
    qi = jnp.arange(w)[:, None]
    kj = jnp.arange(2 * w)[None, :]
    dist = qi + w - kj
    band = (dist >= 0) & (dist <= w)
    valid = band[None] & ((jnp.arange(nb)[:, None, None] > 0) | (kj >= w)[None])
    scores = jnp.where(valid[None, :, None], scores, NEG_INF)
    m = jnp.max(scores, axis=-1, keepdims=True)
    p = jnp.exp(scores - m)
    den = jnp.sum(p, axis=-1, keepdims=True)
    out = jnp.einsum('bnhqk,bnkhd->bnqhd', p / den, vw.astype(jnp.float32))
    lse = (m + jnp.log(den))[..., 0]
    out = (out.reshape(bb, lp, h, dh)[:, :l]
           .reshape(b, dilation, l, h, dh).transpose(0, 2, 1, 3, 4).reshape(b, s, h, dh))
    lse = (lse.transpose(0, 1, 3, 2).reshape(bb, lp, h)[:, :l]
           .reshape(b, dilation, l, h).transpose(0, 2, 1, 3).reshape(b, s, h))
    return out, lse

def _dilated_attention(q, k, v):
    outs, lses = [], []
    for window, dilation in DILATED_PATTERNS:
        o, lse = _dilated_branch(q, k, v, window, dilation)
        outs.append(o)
        lses.append(lse)
    wts = jax.nn.softmax(jnp.stack(lses), axis=0)
    return jnp.einsum('pbsh,pbshd->bshd', wts, jnp.stack(outs))

def _hgrn2(q, f_pre, inp, lb):
    b, s, h, n = q.shape
    dv = inp.shape[-1]
    c = HG_CHUNK
    nc = s // c
    lb = lb.reshape(h, n).astype(jnp.float32)
    f = lb + (1.0 - lb) * jax.nn.sigmoid(f_pre.astype(jnp.float32))
    g = jnp.log(f)
    k = 1.0 - f

    def chunks(t):
        return t.reshape(b, nc, c, h, t.shape[-1]).transpose(0, 3, 1, 2, 4)

    qc, kc, gc, vc = chunks(q.astype(jnp.float32)), chunks(k), chunks(g), chunks(inp.astype(jnp.float32))
    G = jnp.cumsum(gc, axis=3)
    G_last = G[:, :, :, -1:]
    q_dec = qc * jnp.exp(G)
    att = jnp.einsum('bhntk,bhnsk->bhnts', q_dec, kc * jnp.exp(-G))
    att = jnp.where(jnp.tril(jnp.ones((c, c), dtype=bool)), att, 0.0)
    intra = jnp.einsum('bhnts,bhnsv->bhntv', att, vc)
    chunk_state = jnp.einsum('bhnsk,bhnsv->bhnkv', kc * jnp.exp(G_last - G), vc)
    decay = jnp.exp(G_last[:, :, :, 0])

    def step(state, xs):
        dec, upd = xs
        return dec[..., None] * state + upd, state

    _, prev = lax.scan(step, jnp.zeros((b, h, n, dv), jnp.float32),
                       (jnp.moveaxis(decay, 2, 0), jnp.moveaxis(chunk_state, 2, 0)))
    prev = jnp.moveaxis(prev, 0, 2)
    inter = jnp.einsum('bhntk,bhnkv->bhntv', q_dec, prev)
    return (intra + inter).transpose(0, 2, 3, 1, 4).reshape(b, s, h, dv)

def first_inputs(seed: int = 0) -> dict:
    key = jax.random.key(seed)
    ks = jax.random.split(key, 20)
    f32 = jnp.float32

    def nrm(k, shape, fan_in):
        return jax.random.normal(k, shape, f32) * (fan_in ** -0.5)

    def gain(k, shape):
        return 1.0 + 0.02 * jax.random.normal(k, shape, f32)

    return {
        'x': jax.random.normal(ks[0], (BATCH, SEQ, D_MODEL), f32),
        'ffn1_norm': gain(ks[1], (DEPTH, D_MODEL)),
        'ffn1_w1': nrm(ks[2], (DEPTH, D_MODEL, D_FF), D_MODEL),
        'ffn1_w3': nrm(ks[3], (DEPTH, D_MODEL, D_FF), D_MODEL),
        'ffn1_w2': nrm(ks[4], (DEPTH, D_FF, D_MODEL), D_FF),
        'mix_norm': gain(ks[5], (DEPTH, D_MODEL)),
        'w_in': nrm(ks[6], (DEPTH, D_MODEL, IN_COLS), D_MODEL),
        'q_norm': gain(ks[7], (DEPTH, HEAD_DIM)),
        'k_norm': gain(ks[8], (DEPTH, HEAD_DIM)),
        'hg_lb_logits': 0.1 * jax.random.normal(ks[9], (DEPTH + 1, HG_KDIM), f32),
        'hg_out_norm': gain(ks[10], (DEPTH, HG_VDIM)),
        'w_out': nrm(ks[11], (DEPTH, MIX_WIDTH, D_MODEL), MIX_WIDTH),
        'ffn2_norm': gain(ks[12], (DEPTH, D_MODEL)),
        'ffn2_w1': nrm(ks[13], (DEPTH, D_MODEL, D_FF), D_MODEL),
        'ffn2_w3': nrm(ks[14], (DEPTH, D_MODEL, D_FF), D_MODEL),
        'ffn2_w2': nrm(ks[15], (DEPTH, D_FF, D_MODEL), D_FF),
    }

def first_block(x, ffn1_norm, ffn1_w1, ffn1_w3, ffn1_w2, mix_norm, w_in, q_norm, k_norm,
              hg_lb_logits, hg_out_norm, w_out, ffn2_norm, ffn2_w1, ffn2_w3, ffn2_w2):
    b, s, _ = x.shape
    cos, sin = _rope_tables(s)
    lower_bounds = jnp.cumsum(jax.nn.softmax(hg_lb_logits.astype(jnp.float32), axis=0), axis=0)
    split_at = list(np.cumsum(IN_SIZES)[:-1])
    for layer in range(DEPTH):
        x = x + 0.5 * _swiglu(_rms_norm(x, ffn1_norm[layer]),
                              ffn1_w1[layer], ffn1_w3[layer], ffn1_w2[layer])
        h = _rms_norm(x, mix_norm[layer])
        proj = h @ w_in[layer]
        aq, ak, av, hq, hf, hi, hg = jnp.split(proj, split_at, axis=-1)
        aq = _partial_rope(_rms_norm(aq.reshape(b, s, ATTN_HEADS, HEAD_DIM), q_norm[layer]), cos, sin)
        ak = _partial_rope(_rms_norm(ak.reshape(b, s, ATTN_HEADS, HEAD_DIM), k_norm[layer]), cos, sin)
        av = av.reshape(b, s, ATTN_HEADS, HEAD_DIM)
        attn_out = _dilated_attention(aq, ak, av).astype(x.dtype).reshape(b, s, ATTN_WIDTH)
        rec = _hgrn2(hq.reshape(b, s, HG_HEADS, HG_EXPAND), hf.reshape(b, s, HG_HEADS, HG_EXPAND),
                     hi.reshape(b, s, HG_HEADS, HG_VDIM), lower_bounds[layer]).astype(x.dtype)
        rec = _rms_norm(rec, hg_out_norm[layer]) * jax.nn.silu(hg.reshape(b, s, HG_HEADS, HG_VDIM))
        mixed = jnp.concatenate([attn_out, rec.reshape(b, s, HG_WIDTH)], axis=-1)
        x = x + mixed @ w_out[layer]
        x = x + 0.5 * _swiglu(_rms_norm(x, ffn2_norm[layer]),
                              ffn2_w1[layer], ffn2_w3[layer], ffn2_w2[layer])
    return x


DEPTH_2 = 2

CHUNK = 64

D_A = D_MODEL // 2
S5_H = 16
S5_G = D_A // S5_H
S5_P = 64
DT_MIN = 1e-3
DT_MAX = 1e-1
D_B = D_MODEL - D_A
POOL_WINDOWS = (2, 4, 8, 16)
POOL_GROUPS = len(POOL_WINDOWS)
POOL_C = D_B // POOL_GROUPS
SB_HEADS = 16
SB_HEAD_DIM = D_MODEL // SB_HEADS
SB_BLOCK = 128
N_EXPERTS = 16
N_EXPERT_GROUPS = 4
EXPERTS_PER_GROUP = N_EXPERTS // N_EXPERT_GROUPS
TOP_K = 2
D_EXPERT = 512
PLE_DIM = 256
DEEPNORM_ALPHA = (2 * DEPTH_2) ** 0.25
DEEPNORM_BETA = (8 * DEPTH_2) ** -0.25
LN_EPS = 1e-5
N_EVEN = (DEPTH_2 + 1) // 2
N_ODD = DEPTH_2 // 2


F32 = jnp.float32

def layer_norm(x, g, b):
    x32 = x.astype(F32)
    mu = jnp.mean(x32, axis=-1, keepdims=True)
    var = jnp.mean(jnp.square(x32 - mu), axis=-1, keepdims=True)
    return ((x32 - mu) * lax.rsqrt(var + LN_EPS) * g.astype(F32) + b.astype(F32)).astype(x.dtype)

def _complex_linear_combine(e1, e2):
    a1r, a1i, b1r, b1i = e1
    a2r, a2i, b2r, b2i = e2
    ar = a2r * a1r - a2i * a1i
    ai = a2r * a1i + a2i * a1r
    br = a2r * b1r - a2i * b1i + b2r
    bi = a2r * b1i + a2i * b1r + b2i
    return (ar, ai, br, bi)

def s5_mixer(u, lam_re, lam_im, log_dt, b_re, b_im, c_re, c_im, d_skip, w_glu):
    bsz, s, _ = u.shape
    u32 = u.astype(F32).reshape(bsz, s, S5_G, S5_H)
    lam_re = lam_re.astype(F32)
    lam_im = lam_im.astype(F32)
    dt = jnp.exp(log_dt.astype(F32))[:, None]
    mag = jnp.exp(lam_re * dt)
    ang = lam_im * dt
    lb_re = mag * jnp.cos(ang)
    lb_im = mag * jnp.sin(ang)
    den = lam_re * lam_re + lam_im * lam_im
    num_re = lb_re - 1.0
    f_re = (num_re * lam_re + lb_im * lam_im) / den
    f_im = (lb_im * lam_re - num_re * lam_im) / den
    b_re = b_re.astype(F32)
    b_im = b_im.astype(F32)
    bb_re = f_re[..., None] * b_re - f_im[..., None] * b_im
    bb_im = f_re[..., None] * b_im + f_im[..., None] * b_re
    bu_re = jnp.einsum('bsgh,gph->sbgp', u32, bb_re)
    bu_im = jnp.einsum('bsgh,gph->sbgp', u32, bb_im)
    a_re = jnp.broadcast_to(lb_re[None, None], (s, 1, S5_G, S5_P))
    a_im = jnp.broadcast_to(lb_im[None, None], (s, 1, S5_G, S5_P))
    _, _, st_re, st_im = lax.associative_scan(
        _complex_linear_combine, (a_re, a_im, bu_re, bu_im), axis=0)
    y = (jnp.einsum('sbgp,ghp->bsgh', st_re, c_re.astype(F32))
         - jnp.einsum('sbgp,ghp->bsgh', st_im, c_im.astype(F32))
         + d_skip.astype(F32) * u32)
    y = jax.nn.gelu(y.reshape(bsz, s, D_A))
    out = y * jax.nn.sigmoid(y @ w_glu.astype(F32))
    return out.astype(u.dtype)

def pool_mixer(v, pool_w, pool_scale):
    bsz, s, _ = v.shape
    v32 = v.astype(F32).reshape(bsz, s, POOL_GROUPS, POOL_C)
    csum = jnp.cumsum(v32, axis=1)
    t = jnp.arange(s)
    means = []
    for gi, w in enumerate(POOL_WINDOWS):
        c = csum[:, :, gi]
        lagged = jnp.pad(c, ((0, 0), (w, 0), (0, 0)))[:, :s]
        count = jnp.minimum(t + 1, w).astype(F32)[None, :, None]
        means.append((c - lagged) / count)
    pooled = jnp.stack(means, axis=2) - v32
    mixed = jnp.einsum('bsgc,gcd->bsgd', pooled, pool_w.astype(F32))
    return (mixed.reshape(bsz, s, D_B) * pool_scale.astype(F32)).astype(v.dtype)

def stick_breaking_attention(qkv):
    bsz, s, _ = qkv.shape
    q, k, v = jnp.split(qkv.astype(F32), 3, axis=-1)
    to_heads = lambda z: z.reshape(bsz, s, SB_HEADS, SB_HEAD_DIM).transpose(0, 2, 1, 3)
    q, k, v = to_heads(q), to_heads(k), to_heads(v)
    scale = SB_HEAD_DIM ** -0.5
    outs = []
    for blk in range(s // SB_BLOCK):
        q0 = blk * SB_BLOCK
        end = q0 + SB_BLOCK
        z = jnp.einsum('bhqd,bhkd->bhqk', q[:, :, q0:end], k[:, :, :end]) * scale
        t_pos = q0 + jnp.arange(SB_BLOCK)
        s_pos = jnp.arange(end)
        causal = s_pos[None, :] < t_pos[:, None]
        log_keep = jnp.where(causal, jax.nn.log_sigmoid(-z), 0.0)
        log_after = lax.cumsum(log_keep, axis=3, reverse=True) - log_keep
        wts = jnp.where(causal, jnp.exp(jax.nn.log_sigmoid(z) + log_after), 0.0)
        outs.append(jnp.einsum('bhqk,bhkd->bhqd', wts, v[:, :, :end]))
    o = jnp.concatenate(outs, axis=2)
    return o.transpose(0, 2, 1, 3).reshape(bsz, s, D_MODEL).astype(qkv.dtype)

def grouped_moe(x, router_w, router_bias, w1, w3, w2):
    bsz, s, d = x.shape
    xt = x.reshape(-1, d)
    scores = jax.nn.sigmoid((xt @ router_w).astype(F32))
    sel = scores + router_bias.astype(F32)
    grp = sel.reshape(-1, N_EXPERT_GROUPS, EXPERTS_PER_GROUP)
    grp_score = jnp.sum(lax.top_k(grp, TOP_K)[0], axis=-1)
    top_group = jnp.argmax(grp_score, axis=-1)
    in_group = (jnp.arange(N_EXPERTS) // EXPERTS_PER_GROUP)[None, :] == top_group[:, None]
    _, idx = lax.top_k(jnp.where(in_group, sel, -jnp.inf), TOP_K)
    w = jnp.take_along_axis(scores, idx, axis=-1)
    w = w / jnp.sum(w, axis=-1, keepdims=True)
    gates = jnp.sum(jax.nn.one_hot(idx, N_EXPERTS, dtype=F32) * w[..., None], axis=1)
    h = jax.nn.silu(jnp.einsum('td,edf->etf', xt, w1)) * jnp.einsum('td,edf->etf', xt, w3)
    h = h * gates.T[:, :, None].astype(h.dtype)
    y = jnp.einsum('etf,efd->td', h, w2)
    return y.reshape(bsz, s, d).astype(x.dtype)

def second_inputs(seed: int = 0) -> dict:
    key = jax.random.key(seed)
    ks = jax.random.split(key, 32)
    nrm = lambda k, shape, sc: jax.random.normal(k, shape, F32) * sc
    n_idx = jnp.arange(S5_P, dtype=F32)
    return {
        'x': nrm(ks[0], (BATCH, SEQ, D_MODEL), 1.0),
        'p': nrm(ks[1], (DEPTH_2, BATCH, SEQ, PLE_DIM), 1.0),
        'ab_w_in': nrm(ks[2], (N_EVEN, D_MODEL, D_A + D_B), D_MODEL ** -0.5),
        's5_lambda_re': -0.5 + nrm(ks[3], (N_EVEN, S5_G, S5_P), 0.01),
        's5_lambda_im': math.pi * n_idx + nrm(ks[4], (N_EVEN, S5_G, S5_P), 0.01),
        's5_log_dt': jax.random.uniform(ks[5], (N_EVEN, S5_G), F32, math.log(DT_MIN), math.log(DT_MAX)),
        's5_b_re': nrm(ks[6], (N_EVEN, S5_G, S5_P, S5_H), (2 * S5_H) ** -0.5),
        's5_b_im': nrm(ks[7], (N_EVEN, S5_G, S5_P, S5_H), (2 * S5_H) ** -0.5),
        's5_c_re': nrm(ks[8], (N_EVEN, S5_G, S5_H, S5_P), S5_P ** -0.5),
        's5_c_im': nrm(ks[9], (N_EVEN, S5_G, S5_H, S5_P), S5_P ** -0.5),
        's5_d': nrm(ks[10], (N_EVEN, S5_G, S5_H), 1.0),
        's5_w_glu': nrm(ks[11], (N_EVEN, D_A, D_A), D_A ** -0.5),
        'pool_w': nrm(ks[12], (N_EVEN, POOL_GROUPS, POOL_C, POOL_C), POOL_C ** -0.5),
        'pool_scale': 1.0 + nrm(ks[13], (N_EVEN, D_B), 0.1),
        'ab_w_out': nrm(ks[14], (N_EVEN, D_A + D_B, D_MODEL), (D_A + D_B) ** -0.5 * DEEPNORM_BETA),
        'sb_w_qkv': nrm(ks[15], (N_ODD, D_MODEL, 3 * D_MODEL), D_MODEL ** -0.5),
        'sb_w_out': nrm(ks[16], (N_ODD, D_MODEL, D_MODEL), D_MODEL ** -0.5 * DEEPNORM_BETA),
        'ln_mix_g': 1.0 + nrm(ks[17], (DEPTH_2, D_MODEL), 0.01),
        'ln_mix_b': nrm(ks[18], (DEPTH_2, D_MODEL), 0.01),
        'ln_ffn_g': 1.0 + nrm(ks[19], (DEPTH_2, D_MODEL), 0.01),
        'ln_ffn_b': nrm(ks[20], (DEPTH_2, D_MODEL), 0.01),
        'router_w': nrm(ks[21], (D_MODEL, N_EXPERTS), D_MODEL ** -0.5),
        'router_bias': nrm(ks[22], (N_EXPERTS,), 0.01),
        'moe_w1': nrm(ks[23], (DEPTH_2, N_EXPERTS, D_MODEL, D_EXPERT), D_MODEL ** -0.5),
        'moe_w3': nrm(ks[24], (DEPTH_2, N_EXPERTS, D_MODEL, D_EXPERT), D_MODEL ** -0.5),
        'moe_w2': nrm(ks[25], (DEPTH_2, N_EXPERTS, D_EXPERT, D_MODEL), D_EXPERT ** -0.5 * DEEPNORM_BETA),
        'ple_w_proj': nrm(ks[26], (DEPTH_2, PLE_DIM, D_MODEL), PLE_DIM ** -0.5 * DEEPNORM_BETA),
        'ple_w_gate': nrm(ks[27], (DEPTH_2, D_MODEL, D_MODEL), D_MODEL ** -0.5),
    }

def second_block(x, p, ab_w_in, s5_lambda_re, s5_lambda_im, s5_log_dt, s5_b_re, s5_b_im,
              s5_c_re, s5_c_im, s5_d, s5_w_glu, pool_w, pool_scale, ab_w_out,
              sb_w_qkv, sb_w_out, ln_mix_g, ln_mix_b, ln_ffn_g, ln_ffn_b,
              router_w, router_bias, moe_w1, moe_w3, moe_w2, ple_w_proj, ple_w_gate):
    for i in range(DEPTH_2):
        j = i // 2
        if i % 2 == 0:
            h = x @ ab_w_in[j]
            out_a = s5_mixer(h[..., :D_A], s5_lambda_re[j], s5_lambda_im[j], s5_log_dt[j],
                             s5_b_re[j], s5_b_im[j], s5_c_re[j], s5_c_im[j], s5_d[j], s5_w_glu[j])
            out_b = pool_mixer(h[..., D_A:], pool_w[j], pool_scale[j])
            mix = jnp.concatenate([out_a, out_b], axis=-1) @ ab_w_out[j]
        else:
            mix = stick_breaking_attention(x @ sb_w_qkv[j]) @ sb_w_out[j]
        x = layer_norm(DEEPNORM_ALPHA * x + mix, ln_mix_g[i], ln_mix_b[i])
        ple = (p[i] @ ple_w_proj[i]) * jax.nn.sigmoid(x @ ple_w_gate[i])
        ffn = grouped_moe(x, router_w, router_bias, moe_w1[i], moe_w3[i], moe_w2[i])
        x = layer_norm(DEEPNORM_ALPHA * x + ffn + ple, ln_ffn_g[i], ln_ffn_b[i])
    return x


def setup_inputs(seed=0):
    out = dict(first_inputs(seed))
    for name, value in second_inputs(seed + 1).items():
        if name != "x":
            out[name + "_2"] = value
    return out


def reference(
    x, ffn1_norm, ffn1_w1, ffn1_w3, ffn1_w2, mix_norm, w_in, q_norm, k_norm, hg_lb_logits,
    hg_out_norm, w_out, ffn2_norm, ffn2_w1, ffn2_w3, ffn2_w2, p_2, ab_w_in_2, s5_lambda_re_2,
    s5_lambda_im_2, s5_log_dt_2, s5_b_re_2, s5_b_im_2, s5_c_re_2, s5_c_im_2, s5_d_2, s5_w_glu_2,
    pool_w_2, pool_scale_2, ab_w_out_2, sb_w_qkv_2, sb_w_out_2, ln_mix_g_2, ln_mix_b_2,
    ln_ffn_g_2, ln_ffn_b_2, router_w_2, router_bias_2, moe_w1_2, moe_w3_2, moe_w2_2,
    ple_w_proj_2, ple_w_gate_2,
):
    x = first_block(
        x, ffn1_norm, ffn1_w1, ffn1_w3, ffn1_w2, mix_norm, w_in, q_norm, k_norm, hg_lb_logits,
        hg_out_norm, w_out, ffn2_norm, ffn2_w1, ffn2_w3, ffn2_w2,
    )
    return second_block(
        x, p_2, ab_w_in_2, s5_lambda_re_2, s5_lambda_im_2, s5_log_dt_2, s5_b_re_2, s5_b_im_2,
        s5_c_re_2, s5_c_im_2, s5_d_2, s5_w_glu_2, pool_w_2, pool_scale_2, ab_w_out_2,
        sb_w_qkv_2, sb_w_out_2, ln_mix_g_2, ln_mix_b_2, ln_ffn_g_2, ln_ffn_b_2, router_w_2,
        router_bias_2, moe_w1_2, moe_w3_2, moe_w2_2, ple_w_proj_2, ple_w_gate_2,
    )


_drawn_inputs = setup_inputs


def setup_inputs(seed=0):
    import zlib

    import numpy as np

    out = dict(_drawn_inputs(seed))
    spreads = {}
    factors = {'q_norm': 3.985,
     'k_norm': 4.227,
     's5_lambda_re_2': 64.0,
     's5_b_re_2': 3.438,
     'ffn2_norm': 3.438,
     's5_b_im_2': 6.584,
     's5_c_re_2': 2.778,
     's5_c_im_2': 3.234,
     'ln_ffn_g_2': 2.814,
     'ln_ffn_b_2': 2.954}
    for name, (base, spread) in spreads.items():
        noise = np.random.default_rng([zlib.crc32(name.encode()), seed]).standard_normal(out[name].shape)
        drawn = base * np.exp(spread * noise) if base else spread * noise
        out[name] = jnp.asarray(drawn.astype(out[name].dtype))
    for name, factor in factors.items():
        out[name] = (out[name] * factor).astype(out[name].dtype)
    return out
```

```python
from contextlib import ExitStack
import math

import numpy as np
import concourse.bass as bass
from concourse import mybir
from concourse.alu_op_type import AluOpType as ALU

F32 = mybir.dt.float32
I32 = mybir.dt.int32
ACT = mybir.ActivationFunctionType
AX = mybir.AxisListType.X

T = 256
D = 1024
ALPHA = 4 ** 0.25
SLOTS = 6
SCOLS = 2048
TWO_PI = 2 * math.pi
MAGIC = 1.5 * 2.0 ** 23

PARAMS = [("n1", 8), ("nm", 8), ("n2", 8), ("lb", 8), ("hgn", 1), ("qn", 64), ("kn", 64), ("lre", 16),
          ("lim", 16), ("ldt", 16), ("sd", 4), ("ps", 4), ("rb", 16), ("rw", 128), ("bre", 512), ("bim", 512)]
CONSTS = [("ident", 128), ("ones", 128), ("tri", 128), ("strict", 128), ("neg", 128), ("abias", 384),
          ("hgm", 128), ("seg", 256), ("cos", 16), ("sin", 16), ("invc", 64), ("lower", 16)]


def offsets(table):
    at, out = 0, {}
    for name, n in table:
        out[name] = (at, n)
        at += n
    return out, at


class Op:

    def __init__(self, eng, fn, after):
        self.eng, self.fn, self.after = eng, fn, after
        self.wanted = False
        self.sem, self.value = None, None


class Queues:

    def __init__(self):
        self.q = {e: [] for e in ("pe", "act", "dve", "pool", "sp")}

    def put(self, eng, fn, *after):
        flat = []
        for a in after:
            flat += [x for x in a if x is not None] if isinstance(a, (list, tuple)) else [a] if a is not None else []
        for a in flat:
            a.wanted = True
        op = Op(eng, fn, flat)
        self.q[eng].append(op)
        return op

    def dma(self, eng, fn, sem, value, *after):
        op = self.put(eng, fn, *after)
        op.sem, op.value = sem, value
        return op

    def number(self, sems):
        for eng, ops in self.q.items():
            n = 0
            for op in ops:
                if op.sem is None and op.wanted:
                    n += 1
                    op.sem, op.value = sems[eng], n

    def emit(self, eng, handle):
        seen = {}
        for op in self.q[eng]:
            need = {}
            for a in op.after:
                if need.get(a.sem.name, (None, 0))[1] < a.value:
                    need[a.sem.name] = (a.sem, a.value)
            for name, (sem, v) in need.items():
                if seen.get(name, 0) < v:
                    handle.wait_ge(sem, v)
                    seen[name] = v
            ins = op.fn(handle)
            if op.sem is not None:
                ins.then_inc(op.sem, 16 if op.value % 16 == 0 and op.sem.name.startswith("d_") else 1)


def build(nc, a):
    Q = Queues()
    ctx = ExitStack()
    with ctx:
        def sb(name, cols, parts=128, dt=F32):
            return ctx.enter_context(nc.sbuf_tensor(name, [parts, cols], dt))

        def sem(name):
            return ctx.enter_context(nc.semaphore(name))

        ring = sb("ring", SLOTS * SCOLS)
        Xs = sb("Xs", 2048)
        XN = sb("XN", 2048)
        XT = sb("XT", 2048)
        CS = sb("CS", 8192)
        SC = sb("SC", 16640)
        GB = sb("GB", 2048)
        po, pn = offsets(PARAMS)
        co, cn = offsets(CONSTS)
        PR = sb("PR", pn)
        CO = sb("CO", cn)
        HS = sb("HS", 1024)
        HT = sb("HT", 1024)
        SM = sb("SM", 768)
        CM = sb("CM", 1536)
        banks = [ctx.enter_context(nc.psum_tensor(f"pb{i}", [128, 512], F32)) for i in range(8)]
        sems = {e: sem("e_" + e) for e in Q.q}
        slot_sem = [sem(f"d_slot{i}") for i in range(SLOTS)]

        def par(name, lo=0, n=None):
            o, w = po[name]
            return PR[:, o + lo:o + lo + (w - lo if n is None else n)]

        def con(name, lo=0, n=None):
            o, w = co[name]
            return CO[:, o + lo:o + lo + (w - lo if n is None else n)]

        ident = con("ident")
        X3 = Xs[:, :].rearrange("p (t d) -> p t d", t=2)
        XN3 = XN[:, :].rearrange("p (t d) -> p t d", t=2)
        XT3 = XT[:, :].rearrange("p (k t) -> p k t", k=8)

        small_at = [0]

        def small(n):
            at = small_at[0]
            small_at[0] += n
            assert small_at[0] <= 768
            return SM[:, at:at + n]

        def pe(fn, *after):
            return Q.put("pe", fn, *after)

        def act(fn, *after):
            return Q.put("act", fn, *after)

        def dve(fn, *after):
            return Q.put("dve", fn, *after)

        def pool(fn, *after):
            return Q.put("pool", fn, *after)

        n_misc = [0]

        def load(dst, src, *after, eng="sp"):
            n_misc[0] += 1
            return Q.dma(eng, lambda e: e.dma_start(dst, src), sem(f"d_m{n_misc[0]}"), 16, *after)

        slot_free = [None] * SLOTS
        slot_uses = [0] * SLOTS
        n_blocks = [0]

        class Block:
            def __init__(self, src):
                cols = src.shape[-1]
                self.slot = n_blocks[0] % SLOTS
                n_blocks[0] += 1
                s = self.slot
                slot_uses[s] += 1
                self.ap = ring[:, s * SCOLS:s * SCOLS + cols]
                self.here = Q.dma("sp", lambda e: e.dma_start(self.ap, src), slot_sem[s], 16 * slot_uses[s],
                                  slot_free[s])

            def done(self, op):
                slot_free[self.slot] = op

            def view(self, **kw):
                (k, v), = kw.items()
                return self.ap.rearrange(f"p ({k} n) -> p {k} n", **{k: v})

        bank_read = [[] for _ in range(8)]
        turn = [0]

        def bank(first=0):
            turn[0] += 1
            b = first + turn[0] % (8 - first)
            w = bank_read[b]
            bank_read[b] = []
            return b, w

        def mm(e, out, l, r, start, stop, **kw):
            return e.matmul(out, l, r, start=start, stop=stop, **kw)

        l_par = load(PR[:, :], a["params"])
        l_con = load(CO[:, :], a["consts"])
        l_x = load(X3, a["x"])
        c_raw = SC[:, 0:1024]
        l_c = load(c_raw, a["s5c"])

        rs = small(2)
        ss = small(2)

        def transposes(src3, src_ready, weight, xt_read):
            out = []
            for kp in range(4):
                b, w = bank()
                P = banks[b]

                def go(e, kp=kp, P=P):
                    for k in range(2):
                        for t in range(2):
                            i = e.transpose(P[:, k * 256 + t * 128:k * 256 + t * 128 + 128],
                                            src3[:, t, (2 * kp + k) * 128:(2 * kp + k + 1) * 128], ident)
                    return i
                t = pe(go, w, src_ready, l_con)
                if weight is None:
                    dst = XT[:, kp * 512:kp * 512 + 512]
                    f = act if kp % 2 else dve
                    if kp % 2:
                        r = act(lambda e, d=dst, P=P: e.copy(d, P[:, :]), t, xt_read)
                    else:
                        r = dve(lambda e, d=dst, P=P: e.tensor_copy(d, P[:, :]), t, xt_read)
                    out.append(r)
                    bank_read[b] = [r]
                else:
                    for k in range(2):
                        dst, src, wk = XT3[:, 2 * kp + k, :], P[:, k * 256:k * 256 + 256], weight[:, 2 * kp + k:2 * kp + k + 1]
                        if kp % 2:
                            r = act(lambda e, dst=dst, src=src, wk=wk: e.activation(dst, src, ACT.Copy, scale=wk),
                                    t, xt_read, l_par)
                        else:
                            r = dve(lambda e, dst=dst, src=src, wk=wk: e.tensor_scalar(dst, src, wk, None, ALU.mult),
                                    t, xt_read, l_par)
                    out.append(r)
                    bank_read[b] = [r]
            return out

        def rms_transpose(x_ready, weight, xn_free, xt_read):
            ready = []
            for t in range(2):
                s1 = dve(lambda e, t=t: e.tensor_tensor_reduce(XN3[:, t, :], X3[:, t, :], X3[:, t, :], 1.0, 0.0,
                                                               ALU.mult, ALU.add, ss[:, t:t + 1]), x_ready, xn_free)
            s2 = dve(lambda e: e.tensor_scalar(rs, ss, 1.0 / D, 1e-6, ALU.mult, ALU.add), s1)
            s3 = act(lambda e: e.activation(rs, rs, ACT.Sqrt), s2)
            s4 = dve(lambda e: e.reciprocal(rs, rs), s3)
            for t in range(2):
                ready.append(dve(lambda e, t=t: e.tensor_scalar(XN3[:, t, :], X3[:, t, :], rs[:, t:t + 1], None,
                                                                ALU.mult), s4))
            return transposes(XN3, ready, weight, xt_read)

        hs_read = [None] * 4
        ht_read = [None] * 4
        n_chunk = [0]

        def ffn(w13, w2, groups, xt_ready, gates=None):
            acc_free = [x for b in range(4) for x in bank_read[b]]
            pending = []
            total = 2 * groups
            last = [None, None]

            def down(n, c, hT, ready, blk, release):
                def go(e):
                    for t in range(2):
                        for h in range(2):
                            i = mm(e, banks[2 * t + h][:, :], hT[:, t * 128:t * 128 + 128],
                                   blk.view(c=2)[:, c, h * 512:h * 512 + 512], n == 0, n == total - 1)
                    return i
                d = pe(go, ready, blk.here, acc_free if n == 0 else None)
                if release:
                    blk.done(d)
                return d

            for g in range(groups):
                B1 = Block(w13[g, 0])
                B3 = Block(w13[g, 1])
                B2 = Block(w2[g])
                for c in range(2):
                    n = 2 * g + c
                    b, w = bank(4)
                    P = banks[b]

                    def up(e, half, blk, c=c, P=P):
                        W = blk.view(k=8)
                        for k in range(8):
                            i = mm(e, P[:, half * 256:half * 256 + 256], W[:, k, c * 128:c * 128 + 128],
                                   XT3[:, k, :], k == 0, k == 7)
                        return i
                    u1 = pe(lambda e, up=up, B1=B1: up(e, 0, B1), w, B1.here, xt_ready)
                    u2 = pe(lambda e, up=up, B3=B3: up(e, 1, B3), B3.here)
                    if c == 1:
                        B1.done(u1)
                        B3.done(u2)
                        last[1] = u2
                    s = n_chunk[0] % 4
                    n_chunk[0] += 1
                    hs = HS[:, s * 256:s * 256 + 256]
                    hT = HT[:, s * 256:s * 256 + 256]
                    sl = act(lambda e, hs=hs, P=P: e.activation(hs, P[:, 0:256], ACT.Silu), u2, hs_read[s])
                    if gates is not None:
                        gate, g_ready = gates(g // 2)
                        sl = pool(lambda e, hs=hs, gate=gate: e.tensor_tensor(hs, hs, gate, ALU.mult), sl, g_ready)
                    m = dve(lambda e, hs=hs, hT=hT, P=P: e.tensor_tensor(hT, hs, P[:, 256:512], ALU.mult),
                            sl, u2, ht_read[s])
                    hs_read[s] = m
                    bank_read[b] = [m]
                    pending.append((n, c, hT, m, B2, c == 1, s))
                    if len(pending) > 1:
                        p = pending.pop(0)
                        ht_read[p[6]] = down(*p[:6])
            p = pending.pop(0)
            ht_read[p[6]] = d = down(*p[:6])
            return d, last[1]

        def add_acc(scale_x, scale_acc, ready, x_ready=None):
            out = []
            for b in range(4):
                x = X3[:, b // 2, (b % 2) * 512:(b % 2) * 512 + 512]
                if scale_x is None:
                    o = dve(lambda e, x=x, b=b: e.scalar_tensor_tensor(x, banks[b][:, :], scale_acc, x, ALU.mult,
                                                                       ALU.add), ready, x_ready)
                else:
                    o = dve(lambda e, x=x, b=b: e.scalar_tensor_tensor(x, x, scale_x, banks[b][:, :], ALU.mult,
                                                                       ALU.add), ready, x_ready)
                bank_read[b] = [o]
                out.append(o)
            return out

        def down_proj(src, lhs3, ready, first=0, kcount=8):
            free = [x for b in range(first, first + 4) for x in bank_read[b]]
            for g in range(kcount // 2):
                blk = Block(src[g])

                def go(e, g=g, blk=blk):
                    for c in range(2):
                        k = 2 * g + c
                        for t in range(2):
                            for h in range(2):
                                i = mm(e, banks[first + 2 * t + h][:, :], lhs3[:, k, t * 128:t * 128 + 128],
                                       blk.view(c=2)[:, c, h * 512:h * 512 + 512], k == 0, k == kcount - 1)
                    return i
                d = pe(go, blk.here, ready if g == 0 else None, free if g == 0 else None)
                blk.done(d)
            return d

        def proj_T(src, rhs3, ready, evac, kcount=8):
            for g in range(src.shape[0]):
                blk = Block(src[g])
                b, w = bank()
                P = banks[b]

                def go(e, blk=blk, P=P):
                    W = blk.view(k=kcount)
                    for c in range(2):
                        for k in range(kcount):
                            i = mm(e, P[:, c * 256:c * 256 + 256], W[:, k, c * 128:c * 128 + 128], rhs3[:, k, :],
                                   k == 0, k == kcount - 1)
                    return i
                d = pe(go, blk.here, w, ready if g == 0 else None)
                blk.done(d)
                bank_read[b] = evac(g, P, d)
            return d

        def proj_tok(src, ready, evac):
            b0, w0 = bank()
            b1, w1 = bank()
            Bs = [Block(src[0]), Block(src[1])]
            ds = [None, None]
            for half in range(2):
                for t, b in ((0, b0), (1, b1)):
                    def go(e, half=half, t=t, b=b):
                        W = Bs[half].view(k=4)
                        for k in range(4):
                            i = mm(e, banks[b][:, :], XT3[:, 4 * half + k, t * 128:t * 128 + 128], W[:, k, :],
                                   half == 0 and k == 0, half == 1 and k == 3)
                        return i
                    ds[t] = pe(go, Bs[half].here, (w0, w1)[t] if half == 0 else None, ready)
                Bs[half].done(ds[1])
            for t, b in ((0, b0), (1, b1)):
                bank_read[b] = evac(t, banks[b], ds[t])
            return ds[1]

        lre, lim, ldt = par("lre"), par("lim"), par("ldt")
        dt_, mag, ang, kk, rr, sn, sh, cs, den, t1, t2, t3, t4, fre, fim = (small(16) for _ in range(15))
        CS4 = CS[:, :].rearrange("p (j c t) -> p j c t", j=16, c=2)
        cn, sn2 = small(16), small(16)
        o = act(lambda e: e.activation(dt_, ldt, ACT.Exp), l_par)
        o = dve(lambda e: e.tensor_tensor(t1, lre, dt_, ALU.mult), o)
        o_mag = act(lambda e: e.activation(mag, t1, ACT.Exp), o)
        o = dve(lambda e: e.tensor_tensor(ang, lim, dt_, ALU.mult), o)
        o = dve(lambda e: e.tensor_scalar(kk, ang, 1.0 / TWO_PI, MAGIC, ALU.mult, ALU.add), o)
        o = dve(lambda e: e.tensor_scalar(kk, kk, MAGIC, None, ALU.subtract), o)
        o = dve(lambda e: e.scalar_tensor_tensor(rr, kk, -6.28125, ang, ALU.mult, ALU.add), o)
        o = dve(lambda e: e.scalar_tensor_tensor(rr, kk, -(TWO_PI - 6.28125), rr, ALU.mult, ALU.add), o)
        o = dve(lambda e: e.tensor_scalar(rr, rr, -3.1415925, 3.1415925, ALU.max, ALU.min), o)
        o1 = act(lambda e: e.activation(sn, rr, ACT.Sin), o)
        o2 = act(lambda e: e.activation(sh, rr, ACT.Sin, scale=0.5), o)
        o = dve(lambda e: e.tensor_tensor(cs, sh, sh, ALU.mult), o2)
        o_e1 = dve(lambda e: e.tensor_scalar(cs, cs, -2.0, 1.0, ALU.mult, ALU.add), o)
        o = dve(lambda e: e.tensor_tensor(t1, mag, cs, ALU.mult), o_e1, o_mag)
        o = dve(lambda e: e.tensor_scalar(t1, t1, -1.0, None, ALU.add), o)
        o = dve(lambda e: e.tensor_tensor(t2, mag, sn, ALU.mult), o, o1)
        o = dve(lambda e: e.tensor_tensor(den, lre, lre, ALU.mult))
        o = dve(lambda e: e.tensor_tensor(t3, lim, lim, ALU.mult))
        o = dve(lambda e: e.tensor_tensor(den, den, t3, ALU.add), o)
        o = dve(lambda e: e.reciprocal(den, den), o)
        o = dve(lambda e: e.tensor_tensor(fre, t1, lre, ALU.mult), o)
        o = dve(lambda e: e.tensor_tensor(t3, t2, lim, ALU.mult), o)
        o = dve(lambda e: e.tensor_tensor(fre, fre, t3, ALU.add), o)
        o = dve(lambda e: e.tensor_tensor(fre, fre, den, ALU.mult), o)
        o = dve(lambda e: e.tensor_tensor(fim, t2, lre, ALU.mult), o)
        o = dve(lambda e: e.tensor_tensor(t3, t1, lim, ALU.mult), o)
        o = dve(lambda e: e.tensor_tensor(fim, fim, t3, ALU.subtract), o)
        o_f = dve(lambda e: e.tensor_tensor(fim, fim, den, ALU.mult), o)
        craw = [c_raw[:, 512 * i:512 * i + 512].rearrange("p (j h) -> p j h", j=16) for i in range(2)]
        CM3 = [CM[:, 512 * i:512 * i + 512].rearrange("p (j h) -> p j h", j=16) for i in range(3)]
        ctmp = SC[:, 1024:1536].rearrange("p (j h) -> p j h", j=16)

        def bc(x, n):
            return x.unsqueeze(2).to_broadcast([128, 16, n])
        o = pool(lambda e: e.tensor_tensor(CM3[0], craw[0], bc(fre, 32), ALU.mult), o_f, l_c)
        o = pool(lambda e: e.tensor_tensor(ctmp, craw[1], bc(fim, 32), ALU.mult))
        o = pool(lambda e: e.tensor_tensor(CM3[0], CM3[0], ctmp, ALU.subtract), o)
        o = pool(lambda e: e.tensor_scalar(CM3[1], CM3[0], -1.0, 0.0, ALU.mult, ALU.add), o)
        o = pool(lambda e: e.tensor_tensor(CM3[2], craw[0], bc(fim, 32), ALU.mult), o)
        o = pool(lambda e: e.tensor_tensor(ctmp, craw[1], bc(fre, 32), ALU.mult), o)
        o = pool(lambda e: e.tensor_tensor(CM3[2], CM3[2], ctmp, ALU.add), o)
        o_cm = pool(lambda e: e.tensor_scalar(CM3[2], CM3[2], -1.0, 0.0, ALU.mult, ALU.add), o)
        tb = [SC[:, 1536 + 2048 * i:1536 + 2048 * (i + 1)] for i in range(2)]
        o = pool(lambda e: e.memset(CS4[:, :, 0, 0:1], 1.0))
        o = pool(lambda e: e.memset(CS4[:, :, 1, 0:1], 0.0))
        cur = [pool(lambda e: e.tensor_copy(cn, cs), o_e1), pool(lambda e: e.tensor_copy(sn2, sn), o1), o]
        n = 1
        while n < T:
            c0, s0 = CS4[:, :, 0, 0:n], CS4[:, :, 1, 0:n]
            c1, s1 = CS4[:, :, 0, n:2 * n], CS4[:, :, 1, n:2 * n]
            A = tb[0][:, 0:16 * n].rearrange("p (j t) -> p j t", j=16)
            B = tb[1][:, 0:16 * n].rearrange("p (j t) -> p j t", j=16)
            p1 = pool(lambda e, A=A, c0=c0, n=n: e.tensor_tensor(A, c0, bc(cn, n), ALU.mult), cur)
            p2 = pool(lambda e, B=B, s0=s0, n=n: e.tensor_tensor(B, s0, bc(sn2, n), ALU.mult))
            p3 = pool(lambda e, A=A, B=B, c1=c1: e.tensor_tensor(c1, A, B, ALU.subtract), p2)
            p4 = pool(lambda e, A=A, s0=s0, n=n: e.tensor_tensor(A, s0, bc(cn, n), ALU.mult), p3)
            p5 = pool(lambda e, B=B, c0=c0, n=n: e.tensor_tensor(B, c0, bc(sn2, n), ALU.mult), p4)
            p6 = pool(lambda e, A=A, B=B, s1=s1: e.tensor_tensor(s1, A, B, ALU.add), p5)
            q1 = pool(lambda e: e.tensor_tensor(t3, cn, cn, ALU.mult), o_f, p6)
            q2 = pool(lambda e: e.tensor_tensor(t4, sn2, sn2, ALU.mult), q1)
            q3 = pool(lambda e: e.tensor_tensor(sn2, sn2, cn, ALU.mult), q2)
            q4 = pool(lambda e: e.tensor_tensor(cn, t3, t4, ALU.subtract), q3)
            q5 = pool(lambda e: e.tensor_scalar(sn2, sn2, 2.0, 0.0, ALU.mult, ALU.add), q4)
            cur = [q5, p6]
            n *= 2
        tables_ready = cur

        lbv = par("lb").rearrange("p (i h) -> p i h", i=2)
        lm, l0, l1, lb1, lbs = small(4), small(4), small(4), small(4), small(4)
        o = dve(lambda e: e.tensor_tensor(lm, lbv[:, 0, :], lbv[:, 1, :], ALU.max), l_par)
        o0 = dve(lambda e: e.tensor_tensor(l0, lbv[:, 0, :], lm, ALU.subtract), o)
        o1 = dve(lambda e: e.tensor_tensor(l1, lbv[:, 1, :], lm, ALU.subtract), o)
        o = act(lambda e: e.activation(l0, l0, ACT.Exp), o0)
        o = act(lambda e: e.activation(l1, l1, ACT.Exp), o1)
        o = dve(lambda e: e.tensor_tensor(l1, l0, l1, ALU.add), o)
        o = dve(lambda e: e.reciprocal(l1, l1), o)
        o = dve(lambda e: e.tensor_tensor(lbs, l0, l1, ALU.mult), o)
        lb_ready = dve(lambda e: e.tensor_scalar(lb1, lbs, -1.0, 1.0, ALU.mult, ALU.add), o)

        x_ready = [l_x]
        xt = rms_transpose(x_ready, par("n1"), None, None)
        d, xt_read = ffn(a["ffn1_w13"], a["ffn1_w2"], 11, xt)
        x_ready = add_acc(None, 0.5, d)

        xt = rms_transpose(x_ready, par("nm"), xt, xt_read)
        at = [0]

        def carve(n):
            r = SC[:, at[0]:at[0] + n]
            at[0] += n
            assert at[0] <= 16640, at
            return r

        F, Gt, G, E1, E2 = (carve(1024) for _ in range(5))
        qk = [carve(1024), carve(1024)]
        V, HI, SHG = carve(1024), carve(1024), carve(1024)
        qkT = [carve(1024), carve(1024)]
        attS, ksT = HS[:, :], HT[:, :]
        prev = carve(1536)
        NP = 3
        PB = [carve(384) for _ in range(NP)]
        PT = [carve(384) for _ in range(NP)]
        rope_t = carve(512)
        sc_free = tables_ready + [o_cm]
        z_att = pool(lambda e: e.memset(attS, 0.0), sc_free, d)

        f_done = []

        def evac_f(g, P, d):
            r = act(lambda e: e.activation(F[:, g * 512:g * 512 + 512], P[:, :], ACT.Sigmoid), d, sc_free)
            f_done.append(r)
            return [r]
        proj_T(a["w_hf"], XT3, xt, evac_f)
        fg = []
        for h in range(4):
            fh = F[:, h * 256:h * 256 + 256]
            fg.append(dve(lambda e, fh=fh, h=h: e.tensor_scalar(fh, fh, lb1[:, h:h + 1], lbs[:, h:h + 1], ALU.mult,
                                                                ALU.add), f_done[h // 2], lb_ready))
        lg = act(lambda e: e.activation(Gt, F, ACT.Ln), fg)
        kd = dve(lambda e: e.tensor_scalar(F, F, -1.0, 1.0, ALU.mult, ALU.add), lg)
        for h in range(4):
            sl = slice(h * 256, h * 256 + 256)
            sc = dve(lambda e, sl=sl: e.tensor_tensor_scan(G[:, sl], con("seg"), Gt[:, sl], 0.0, ALU.mult, ALU.add),
                     lg, l_con)
        G16 = G.rearrange("p (c t) -> p c t", t=64)
        Gt16 = Gt.rearrange("p (c t) -> p c t", t=64)
        gl = G16[:, :, 63:64]
        df = dve(lambda e: e.tensor_tensor(Gt16, gl.to_broadcast([128, 16, 64]), G16, ALU.subtract), sc)
        e1 = act(lambda e: e.activation(E1, G, ACT.Exp), sc)
        e2 = act(lambda e: e.activation(E2, G, ACT.Exp, scale=-1.0), sc)
        dec = small(16)
        e3 = act(lambda e: e.activation(dec.unsqueeze(2), gl, ACT.Exp), sc)
        e4 = act(lambda e: e.activation(Gt, Gt, ACT.Exp), df)
        k_dec = dve(lambda e: e.tensor_tensor(E2, E2, F, ALU.mult), e2, kd)
        k_st = dve(lambda e: e.tensor_tensor(Gt, Gt, F, ALU.mult), e4)
        q_dec = []

        def evac_q(g, P, d):
            s = E1[:, g * 512:g * 512 + 512]
            r = dve(lambda e: e.tensor_tensor(s, s, P[:, :], ALU.mult), d, e1)
            q_dec.append(r)
            return [r]
        proj_T(a["w_hq"], XT3, None, evac_q)

        norm_w = [par("qn"), par("kn")]
        hss = [small(16), small(16)]
        att_ready = [[], []]
        cosv = con("cos").rearrange("p (t i) -> p t i", t=2)
        sinv = con("sin").rearrange("p (t i) -> p t i", t=2)
        rope_free = [None]
        for i in range(2):
            q4 = qk[i].rearrange("p (t h d) -> p t h d", t=2, h=8)
            hs3 = hss[i].rearrange("p (t h) -> p t h", t=2)

            def evac(t, P, d, i=i, q4=q4, hs3=hs3):
                Ph = P[:, :].rearrange("p (h d) -> p h d", h=8)
                sq = act(lambda e: e.activation(q4[:, t, :, :], Ph, ACT.Square), d, sc_free)
                s = dve(lambda e: e.tensor_reduce(hs3[:, t, :], q4[:, t, :, :], AX, ALU.add), sq)
                s = dve(lambda e: e.tensor_scalar(hs3[:, t, :], hs3[:, t, :], 1.0 / 64, 1e-6, ALU.mult, ALU.add), s)
                s = act(lambda e: e.activation(hs3[:, t, :], hs3[:, t, :], ACT.Sqrt), s)
                s = dve(lambda e: e.reciprocal(hs3[:, t, :], hs3[:, t, :]), s)
                m = dve(lambda e: e.tensor_tensor(q4[:, t, :, :], Ph,
                                                  hs3[:, t, :].unsqueeze(2).to_broadcast([128, 8, 64]), ALU.mult), s)
                w = pool(lambda e: e.tensor_tensor(q4[:, t, :, :], q4[:, t, :, :],
                                                   norm_w[i].unsqueeze(1).to_broadcast([128, 8, 64]), ALU.mult), m)
                R = [rope_t[:, 64 * j:64 * j + 64].rearrange("p (h i) -> p h i", h=8) for j in range(4)]
                c = cosv[:, t, :].unsqueeze(1).to_broadcast([128, 8, 8])
                s_ = sinv[:, t, :].unsqueeze(1).to_broadcast([128, 8, 8])
                x1, x2 = q4[:, t, :, 0:8], q4[:, t, :, 8:16]
                r = pool(lambda e: e.tensor_tensor(R[0], x1, c, ALU.mult), w, rope_free[0])
                r = pool(lambda e: e.tensor_tensor(R[1], x2, s_, ALU.mult))
                r = pool(lambda e: e.tensor_tensor(R[2], x1, s_, ALU.mult))
                r = pool(lambda e: e.tensor_tensor(R[3], x2, c, ALU.mult))
                r = pool(lambda e: e.tensor_tensor(x1, R[0], R[1], ALU.subtract), r)
                r = pool(lambda e: e.tensor_tensor(x2, R[2], R[3], ALU.add))
                rope_free[0] = r
                att_ready[i].append(r)
                return [m]
            proj_tok(a["w_tok"][i], None, evac)

        keep = {}

        def evac_to(buf, key, func):
            keep[key] = []

            def evac(t, P, d):
                dst = buf[:, t * 512:t * 512 + 512]
                r = act(lambda e: e.activation(dst, P[:, :], func), d, sc_free)
                keep[key].append(r)
                return [r]
            return evac
        proj_tok(a["w_tok"][2], None, evac_to(V, "v", ACT.Copy))
        proj_tok(a["w_tok"][3], None, evac_to(HI, "hi", ACT.Copy))
        p_last = proj_tok(a["w_tok"][4], None, evac_to(SHG, "hg", ACT.Silu))

        mixT = XT3

        HI3 = HI.rearrange("p (t d) -> p t d", t=2)
        SHG3 = SHG.rearrange("p (t d) -> p t d", t=2)
        E1h = E1.rearrange("p (h t) -> p h t", h=4)
        E2h = E2.rearrange("p (h t) -> p h t", h=4)
        Kst = Gt.rearrange("p (h t) -> p h t", h=4)
        att8 = attS.rearrange("p (i t) -> p i t", i=8)
        ks8 = ksT.rearrange("p (i t) -> p i t", i=8)
        prv = prev.rearrange("p (c h v) -> p c h v", c=3, h=4)
        hgm = con("hgm").bitcast(I32)
        att_done, ks_done = [], []
        for h in range(4):
            b, w = bank()
            P = banks[b]

            def go(e, h=h, P=P):
                for t in range(2):
                    s = slice(t * 128, t * 128 + 128)
                    mm(e, P[:, s], E2h[:, h, s], E1h[:, h, s], True, True)
                for t in range(2):
                    i = e.transpose(P[:, 256 + t * 128:384 + t * 128], Kst[:, h, t * 128:t * 128 + 128], ident)
                return i
            t = pe(go, w, q_dec, k_dec, k_st)
            rd = []
            for tt in range(2):
                rd.append(dve(lambda e, h=h, tt=tt, P=P: e.copy_predicated(
                    att8[:, 2 * h + tt, :], hgm, P[:, tt * 128:tt * 128 + 128]), t, z_att))
            att_done.append(rd[-1])
            k = act(lambda e, h=h, P=P: e.copy(ksT[:, h * 256:h * 256 + 256], P[:, 256:512]), rd[-1], sc_free)
            ks_done.append(k)
            bank_read[b] = rd + [k]
        st_done = [None] * 4
        for c in range(3):
            b, w = bank()
            P = banks[b]

            def go(e, c=c, P=P):
                r = slice((c % 2) * 64, (c % 2) * 64 + 64)
                for h in range(4):
                    i = mm(e, P[:, h * 128:h * 128 + 128], ks8[r, 2 * h + c // 2, :],
                           HI3[r, c // 2, h * 128:h * 128 + 128], True, True)
                return i
            t = pe(go, w, ks_done, keep["hi"])
            if c == 0:
                s = act(lambda e, P=P: e.copy(prev[:, 0:512], P[:, :]), t, sc_free)
            else:
                for h in range(4):
                    s_ = dve(lambda e, c=c, h=h, P=P: e.scalar_tensor_tensor(
                        prv[:, c, h, :], prv[:, c - 1, h, :], dec[:, 4 * h + c:4 * h + c + 1],
                        P[:, h * 128:h * 128 + 128], ALU.mult, ALU.add), t, s if h == 0 else None, e3)
                s = s_
            st_done[c + 1] = s
            bank_read[b] = [s]
        rss = small(8)
        rec_banks = []
        for tt in range(2):
            b, w = bank()
            P = banks[b]

            def go(e, tt=tt, P=P):
                for h in range(4):
                    hv = slice(h * 128, h * 128 + 128)
                    i = mm(e, P[:, hv], att8[:, 2 * h + tt, :], HI3[:, tt, hv], True, False, skip_group_check=True)
                    for c in (2 * tt, 2 * tt + 1):
                        if c:
                            i = mm(e, P[(c % 2) * 64:(c % 2) * 64 + 64, hv], E1h[:, h, c * 64:c * 64 + 64],
                                   prv[:, c - 1, h, :], False, c % 2 == 1, skip_group_check=True)
                return i
            t = pe(go, w, att_done, st_done[2 * tt + 1], keep["hi"])
            for h in range(4):
                hv = slice(h * 128, h * 128 + 128)
                sq = act(lambda e, tt=tt, h=h, P=P, hv=hv: e.activation(
                    XN3[:, tt, hv], P[:, hv], ACT.Square, accum_out=rss[:, 4 * tt + h:4 * tt + h + 1]), t)
            rec_banks.append((b, P, sq))
        s = dve(lambda e: e.tensor_scalar(rss, rss, 1.0 / 128, 1e-6, ALU.mult, ALU.add), [r[2] for r in rec_banks])
        s = act(lambda e: e.activation(rss, rss, ACT.Sqrt), s)
        s_r = dve(lambda e: e.reciprocal(rss, rss), s)
        rec_done = []
        for tt in range(2):
            b, P, _ = rec_banks[tt]
            for h in range(4):
                hv = slice(h * 128, h * 128 + 128)
                s = dve(lambda e, tt=tt, h=h, P=P, hv=hv: e.scalar_tensor_tensor(
                    XN3[:, tt, hv], P[:, hv], rss[:, 4 * tt + h:4 * tt + h + 1], SHG3[:, tt, hv], ALU.mult,
                    ALU.mult), s_r, keep["hg"])
            bank_read[b] = [s]
            rec_done.append(s)
        mix_ready = []

        def rec_transposes():
            for hp in range(2):
                b, w = bank()
                P = banks[b]

                def go(e, hp=hp, P=P):
                    for k in range(2):
                        for t in range(2):
                            h = 2 * hp + k
                            i = e.transpose(P[:, k * 256 + t * 128:k * 256 + t * 128 + 128],
                                            XN3[:, t, h * 128:h * 128 + 128], ident)
                    return i
                t = pe(go, w, rec_done)
                r = act(lambda e, hp=hp, P=P: e.activation(XT[:, (4 + 2 * hp) * 256:(6 + 2 * hp) * 256], P[:, :],
                                                           ACT.Copy, scale=par("hgn")), t, p_last)
                bank_read[b] = [r]
                mix_ready.append(r)

        qT = [x.rearrange("p (g t) -> p g t", g=4) for x in qkT]
        qkt_ready = []
        for i in range(2):
            q3 = qk[i].rearrange("p (t d) -> p t d", t=2)
            for gp in range(2):
                b, w = bank()
                P = banks[b]

                def go(e, q3=q3, gp=gp, P=P):
                    for k in range(2):
                        for t in range(2):
                            g = 2 * gp + k
                            i = e.transpose(P[:, k * 256 + t * 128:k * 256 + t * 128 + 128],
                                            q3[:, t, g * 128:g * 128 + 128], ident)
                    return i
                t = pe(go, w, att_ready[i])
                r = act(lambda e, i=i, gp=gp, P=P: e.copy(qkT[i][:, gp * 512:gp * 512 + 512], P[:, :]), t, sc_free)
                bank_read[b] = [r]
                qkt_ready.append(r)
        V3 = V.rearrange("p (t d) -> p t d", t=2)
        abias = con("abias")
        nmax, aden = small(16), small(16)
        pb_free, pt_free = [None] * NP, [None] * NP
        heads = []

        def scores(h):
            r = slice((h % 2) * 64, (h % 2) * 64 + 64)
            hp = h // 2
            b, w = bank()
            P = banks[b]

            def go(e):
                mm(e, P[:, 0:128], qT[0][r, hp, 0:128], qT[1][r, hp, 0:128], True, True)
                return mm(e, P[:, 128:384], qT[0][r, hp, 128:256], qT[1][r, hp, :], True, True)
            t = pe(go, w, qkt_ready)
            p = PB[h % NP]
            s = dve(lambda e: e.scalar_tensor_tensor(p, P[:, 0:384], 0.125, abias, ALU.mult, ALU.add), t,
                    pb_free[h % NP], sc_free)
            bank_read[b] = [s]
            m0 = dve(lambda e: e.tensor_reduce(nmax[:, 2 * h:2 * h + 1], p[:, 0:128], AX, ALU.max, negate=True), s)
            m1 = dve(lambda e: e.tensor_reduce(nmax[:, 2 * h + 1:2 * h + 2], p[:, 128:384], AX, ALU.max,
                                               negate=True), s)
            x0 = act(lambda e: e.activation(p[:, 0:128], p[:, 0:128], ACT.Exp, bias=nmax[:, 2 * h:2 * h + 1],
                                            accum_out=aden[:, 2 * h:2 * h + 1]), m0)
            x1 = act(lambda e: e.activation(p[:, 128:384], p[:, 128:384], ACT.Exp, bias=nmax[:, 2 * h + 1:2 * h + 2],
                                            accum_out=aden[:, 2 * h + 1:2 * h + 2]), m1)
            s = dve(lambda e: e.reciprocal(aden[:, 2 * h:2 * h + 2], aden[:, 2 * h:2 * h + 2]), x0, x1)
            n0 = dve(lambda e: e.tensor_scalar(p[:, 0:128], p[:, 0:128], aden[:, 2 * h:2 * h + 1], None, ALU.mult), s)
            n1 = dve(lambda e: e.tensor_scalar(p[:, 128:384], p[:, 128:384], aden[:, 2 * h + 1:2 * h + 2], None,
                                               ALU.mult), s)
            return n1

        def turn_p(h, ready):
            p = PB[h % NP]
            b, w = bank()
            P = banks[b]

            def go(e):
                for j in range(3):
                    i = e.transpose(P[:, j * 128:j * 128 + 128], p[:, j * 128:j * 128 + 128], ident)
                return i
            t = pe(go, w, ready)
            pb_free[h % NP] = t
            r = act(lambda e: e.copy(PT[h % NP], P[:, 0:384]), t, pt_free[h % NP], sc_free)
            bank_read[b] = [r]
            return r

        pv_bank = [None]

        def pv(h, ready):
            if h % 2 == 0:
                pv_bank[0] = bank()
            b, w = pv_bank[0]
            P = banks[b]
            o_ = slice((h % 2) * 64, (h % 2) * 64 + 64)
            hv = slice(h * 64, h * 64 + 64)
            p = PT[h % NP]

            def go(e):
                mm(e, P[o_, 0:128], V3[:, 0, hv], p[:, 0:128], True, True)
                mm(e, P[o_, 128:256], V3[:, 0, hv], p[:, 128:256], True, False)
                return mm(e, P[o_, 128:256], V3[:, 1, hv], p[:, 256:384], False, True)
            t = pe(go, w if h % 2 == 0 else None, ready, keep["v"])
            pt_free[h % NP] = t
            if h % 2:
                r = act(lambda e: e.copy(mixT[:, h // 2, :], P[:, 0:256]), t, p_last)
                bank_read[b] = [r]
                mix_ready.append(r)

        sc_r, tp_r = {}, {}
        for i in range(8 + 2):
            if i < 8:
                sc_r[i] = scores(i)
            if 1 <= i <= 8:
                tp_r[i - 1] = turn_p(i - 1, sc_r[i - 1])
            if i >= 2:
                pv(i - 2, tp_r[i - 2])
            if i == 3:
                rec_transposes()
        d = down_proj(a["w_out"], mixT, mix_ready)
        x_ready = add_acc(None, 1.0, d)

        xt = rms_transpose(x_ready, par("n2"), None, d)
        d, xt_read = ffn(a["ffn2_w13"], a["ffn2_w2"], 11, xt)
        x_ready = add_acc(None, 0.5, d)

        gb_free = [None]
        bst = small(24)
        mv = small(4)
        rstd = small(2)

        def layer_norm(i, x_ready):
            l_g = load(GB[:, 0:1024], a["ln_g"][i].partition_broadcast(128), gb_free)
            l_b = load(GB[:, 1024:2048], a["ln_b"][i].partition_broadcast(128), gb_free)
            st = bst.rearrange("p (t h s) -> p t h s", t=2, h=2)
            mv2 = mv.rearrange("p (t s) -> p t s", t=2)
            for t in range(2):
                for h in range(2):
                    s = dve(lambda e, t=t, h=h: e.bn_stats(st[:, t, h, :], X3[:, t, h * 512:h * 512 + 512]),
                            x_ready)
            for t in range(2):
                s_ = dve(lambda e, t=t: e.bn_aggr(mv2[:, t, :], st[:, t, :, :]), s)
            s = dve(lambda e: e.tensor_scalar(rstd, mv2[:, :, 1], 1e-5, None, ALU.add), s_)
            s = act(lambda e: e.activation(rstd, rstd, ACT.Sqrt), s)
            s = dve(lambda e: e.reciprocal(rstd, rstd), s)
            out = []
            for t in range(2):
                n_ = dve(lambda e, t=t: e.tensor_scalar(X3[:, t, :], X3[:, t, :], mv2[:, t, 0:1], rstd[:, t:t + 1],
                                                        ALU.subtract, ALU.mult), s)
                m_ = dve(lambda e, t=t: e.tensor_tensor(X3[:, t, :], X3[:, t, :], GB[:, 0:1024], ALU.mult), n_, l_g)
                out.append(pool(lambda e, t=t: e.tensor_tensor(X3[:, t, :], X3[:, t, :], GB[:, 1024:2048], ALU.add),
                                m_, l_b))
            gb_free[0] = out[1]
            return out

        def state_space(xt, xt_read_list):
            at[0] = 0
            uT, vT, cat, yg = carve(1024), carve(1024), carve(2048), carve(1024)
            pa, pb_ = carve(1024), carve(1024)
            NB = 2
            BU = [carve(512) for _ in range(NB)]
            PA = [carve(512) for _ in range(NB)]
            PBB = [carve(512) for _ in range(NB)]
            WW = [carve(512) for _ in range(NB)]
            ZZ = [carve(512) for _ in range(NB)]
            P1 = [carve(512) for _ in range(NB)]
            P2 = [carve(512) for _ in range(NB)]
            cat3 = cat.rearrange("p (k t) -> p k t", k=8)
            uT3 = uT.rearrange("p (k t) -> p k t", k=4)
            vT3 = vT.rearrange("p (k t) -> p k t", k=4)
            yg3 = yg.rearrange("p (k t) -> p k t", k=4)
            got = {}

            def evac(g, P, d):
                dst = (uT, vT)[g // 2][:, (g % 2) * 512:(g % 2) * 512 + 512]
                got[g] = act(lambda e: e.copy(dst, P[:, :]), d)
                return [got[g]]
            p_last = proj_T(a["ab_in"], XT3, xt, evac)
            pb4 = [x.rearrange("p (k t) -> p k t", k=4) for x in (pa, pb_)]
            src, ready = vT3, [got[2], got[3]]
            level = []
            for l in range(4):
                s, dst = 1 << l, pb4[l % 2]
                c1 = pool(lambda e, l=l, s=s, dst=dst, src=src: e.tensor_copy(dst[:, l:, 0:s], src[:, l:, 0:s]), ready)
                c2 = pool(lambda e, l=l, s=s, dst=dst, src=src: e.tensor_tensor(
                    dst[:, l:, s:], src[:, l:, s:], src[:, l:, 0:T - s], ALU.add))
                m1 = pool(lambda e, l=l, dst=dst: e.tensor_tensor(
                    dst[:, l, 0:16], dst[:, l, 0:16], con("invc", 16 * l, 16), ALU.mult), c2)
                m2 = pool(lambda e, l=l, dst=dst: e.tensor_scalar(
                    dst[:, l, 16:], dst[:, l, 16:], 0.5 ** (l + 1), 0.0, ALU.mult, ALU.add))
                m3 = pool(lambda e, l=l, dst=dst: e.tensor_tensor(yg3[:, l, :], dst[:, l, :], vT3[:, l, :],
                                                                  ALU.subtract), m2)
                level.append(m3)
                src, ready = dst, [m3]
            blk = Block(a["pool_w"])
            pw = blk.view(k=4)
            pool_done = []
            for gp in range(2):
                b, w = bank()
                P = banks[b]

                def go(e, gp=gp, P=P):
                    for k in range(2):
                        g = 2 * gp + k
                        i = mm(e, P[:, k * 256:k * 256 + 256], pw[:, g, :], yg3[:, g, :], True, True)
                    return i
                t = pe(go, w, blk.here, level)
                r = []
                for k in range(2):
                    g = 2 * gp + k
                    r.append(act(lambda e, g=g, k=k, P=P: e.activation(
                        cat3[:, 4 + g, :], P[:, k * 256:k * 256 + 256], ACT.Copy, scale=par("ps", g, 1)), t))
                bank_read[b] = r
                pool_done += r
            blk.done(t)
            bre = par("bre").rearrange("p (q n) -> p q n", q=4)
            bim = par("bim").rearrange("p (q n) -> p q n", q=4)
            free = [dict() for _ in range(NB)]
            y_bank = [None]
            yg_done = []
            stage = []

            def first(j):
                q, r = j // 4, slice(32 * (j % 4), 32 * (j % 4) + 32)
                f = free[j % NB]
                b, w = bank()
                P = banks[b]

                def go(e):
                    mm(e, P[:, 0:256], bre[r, q, :], uT3[r, q, :], True, True)
                    return mm(e, P[:, 256:512], bim[r, q, :], uT3[r, q, :], True, True)
                t = pe(go, w, got[0], got[1])
                bu, pA, pB, ww, zz, p1, p2 = (x[j % NB] for x in (BU, PA, PBB, WW, ZZ, P1, P2))
                csj = CS[:, 512 * j:512 * j + 512]
                cj, sj = csj[:, 0:256], csj[:, 256:512]
                cp = act(lambda e: e.copy(bu, P[:, :]), t, f.get("bu"))
                m1 = dve(lambda e: e.tensor_tensor(pA, P[:, :], csj, ALU.mult), cp, f.get("pA"), tables_ready)
                bank_read[b] = [cp, m1]
                m2 = pool(lambda e: e.tensor_tensor(pB[:, 0:256], bu[:, 256:512], cj, ALU.mult), cp)
                m3 = pool(lambda e: e.tensor_tensor(pB[:, 256:512], bu[:, 0:256], sj, ALU.mult))
                f["bu"] = m3
                w1 = dve(lambda e: e.tensor_tensor(ww[:, 0:256], pA[:, 0:256], pA[:, 256:512], ALU.add), m1,
                         f.get("ww"))
                f["pA"] = w1
                w2 = pool(lambda e: e.tensor_tensor(ww[:, 256:512], pB[:, 0:256], pB[:, 256:512], ALU.subtract),
                          m3, f.get("ww"))
                rj = mag[:, j:j + 1].to_broadcast([128, 256])
                z1 = dve(lambda e: e.tensor_tensor_scan(zz[:, 0:256], rj, ww[:, 0:256], 0.0, ALU.mult, ALU.add), w1,
                         f.get("zz"))
                z2 = dve(lambda e: e.tensor_tensor_scan(zz[:, 256:512], rj, ww[:, 256:512], 0.0, ALU.mult, ALU.add),
                         w2)
                f["ww"] = z2
                a1 = dve(lambda e: e.tensor_tensor(p1, zz, csj, ALU.mult), z2, f.get("pe"))
                a2 = pool(lambda e: e.tensor_tensor(p2[:, 0:256], zz[:, 0:256], sj, ALU.mult), z2, f.get("pe"))
                a3 = pool(lambda e: e.tensor_tensor(p2[:, 256:512], zz[:, 256:512], cj, ALU.mult))
                f["zz"] = [a1, a3]
                return [a1, a3]

            def second(j, ready):
                q = j // 4
                if j % 4 == 0:
                    y_bank[0] = bank()
                b, w = y_bank[0]
                P = banks[b]
                o_ = slice(32 * (j % 4), 32 * (j % 4) + 32)
                p1, p2 = P1[j % NB], P2[j % NB]

                def go(e):
                    mm(e, P[o_, 0:256], CM3[0][:, j, :], p1[:, 0:256], True, False)
                    mm(e, P[o_, 0:256], CM3[1][:, j, :], p1[:, 256:512], False, False)
                    mm(e, P[o_, 0:256], CM3[2][:, j, :], p2[:, 0:256], False, False)
                    return mm(e, P[o_, 0:256], CM3[2][:, j, :], p2[:, 256:512], False, True)
                t = pe(go, w if j % 4 == 0 else None, ready)
                free[j % NB]["pe"] = t
                if j % 4 == 3:
                    s = dve(lambda e: e.scalar_tensor_tensor(yg3[:, q, :], uT3[:, q, :], par("sd", q, 1), P[:, 0:256],
                                                             ALU.mult, ALU.add), t, pool_done)
                    bank_read[b] = [s]
                    yg_done.append(act(lambda e: e.activation(yg3[:, q, :], yg3[:, q, :], ACT.Gelu_apprx_tanh), s))
            for j in range(17):
                if j < 16:
                    if y_bank[0] is not None and (turn[0] + 1) % 8 == y_bank[0][0]:
                        turn[0] += 1
                    stage.append(first(j))
                if j >= 1:
                    if (j - 1) % 4 == 0:
                        y_bank[0] = None
                    second(j - 1, stage[j - 1])
            blk = Block(a["w_glu"])
            wg = blk.view(k=4)
            cat_done = list(pool_done)
            for mp in range(2):
                b, w = bank()
                P = banks[b]

                def go(e, mp=mp, P=P):
                    for c in range(2):
                        m = 2 * mp + c
                        for k in range(4):
                            i = mm(e, P[:, c * 256:c * 256 + 256], wg[:, k, m * 128:m * 128 + 128], yg3[:, k, :],
                                   k == 0, k == 3)
                    return i
                t = pe(go, w, blk.here, yg_done)
                dst = cat[:, mp * 512:mp * 512 + 512]
                s = act(lambda e, dst=dst, P=P: e.activation(dst, P[:, :], ACT.Sigmoid), t)
                bank_read[b] = [s]
                cat_done.append(dve(lambda e, dst=dst, mp=mp: e.tensor_tensor(
                    dst, dst, yg[:, mp * 512:mp * 512 + 512], ALU.mult), s))
            blk.done(t)
            return down_proj(a["ab_out"], cat3, cat_done)

        def stick_breaking(xt):
            at[0] = 0
            qT, kT, V, oT = carve(2048), carve(2048), carve(2048), carve(2048)
            NB = 2
            ZS = [carve(384) for _ in range(NB)]
            EE = [carve(384) for _ in range(NB)]
            LL = [carve(384) for _ in range(NB)]
            WW = [carve(384) for _ in range(NB)]
            q3 = qT.rearrange("p (k t) -> p k t", k=8)
            k3 = kT.rearrange("p (k t) -> p k t", k=8)
            o3 = oT.rearrange("p (k t) -> p k t", k=8)
            V3 = V.rearrange("p (t d) -> p t d", t=2)
            got = {"q": [], "k": [], "v": []}

            def evac_q(g, P, d):
                r = act(lambda e: e.activation(qT[:, g * 512:g * 512 + 512], P[:, :], ACT.Copy, scale=0.125), d)
                got["q"].append(r)
                return [r]

            def evac_k(g, P, d):
                r = dve(lambda e: e.tensor_copy(kT[:, g * 512:g * 512 + 512], P[:, :]), d)
                got["k"].append(r)
                return [r]
            proj_T(a["sb_q"], XT3, xt, evac_q)
            proj_T(a["sb_k"], XT3, xt, evac_k)
            for h in range(2):
                def evac_v(t, P, d, h=h):
                    r = act(lambda e: e.copy(V3[:, t, h * 512:h * 512 + 512], P[:, :]), d)
                    got["v"].append(r)
                    return [r]
                proj_tok(a["sb_v"][h], xt, evac_v)
            tri, ones = con("tri"), con("ones")
            zf, wf, lf = [None] * NB, [None] * NB, [None] * NB
            strict2 = con("strict").unsqueeze(1).to_broadcast([128, 2, 128])
            neg2 = con("neg").unsqueeze(1).to_broadcast([128, 2, 128])

            def diag(x):
                return x[:, 0:384].rearrange("p (c t) -> p c t", c=3)[:, 0:3:2, :]

            def head_a(h):
                r, hp, i = slice((h % 2) * 64, (h % 2) * 64 + 64), h // 2, h % NB
                b, w = bank()
                P = banks[b]

                def go(e):
                    mm(e, P[:, 0:256], k3[r, hp, 0:128], q3[r, hp, :], True, True)
                    return mm(e, P[:, 256:384], k3[r, hp, 128:256], q3[r, hp, 128:256], True, True)
                t = pe(go, w, got["q"], got["k"])
                z, ee, ll = ZS[i], EE[i], LL[i]
                c = dve(lambda e: e.tensor_copy(z, P[:, 0:384]), t, zf[i])
                x = act(lambda e: e.activation(ee, z, ACT.Abs), c, lf[i])
                bank_read[b] = [c]
                x = act(lambda e: e.activation(ee, ee, ACT.Exp, scale=-1.0), x)
                x = act(lambda e: e.activation(ee, ee, ACT.Ln, bias=1.0), x)
                l = dve(lambda e: e.scalar_tensor_tensor(ll, z, 0.0, ee, ALU.max, ALU.add), x, c, lf[i])
                m = pool(lambda e: e.tensor_tensor(diag(ll), diag(ll), strict2, ALU.mult), l)
                return m

            def head_b(h, ready):
                i = h % NB
                b, w = bank()
                P = banks[b]
                z, ll, ww = ZS[i], LL[i], WW[i]

                def go(e):
                    mm(e, P[:, 256:384], tri, ll[:, 256:384], True, True)
                    mm(e, P[:, 0:256], tri, ll[:, 0:256], True, False, skip_group_check=True)
                    return mm(e, P[:, 128:256], ones, ll[:, 256:384], False, True, skip_group_check=True)
                t = pe(go, w, ready)
                lf[i] = t
                s = dve(lambda e: e.tensor_tensor(ww, z, P[:, 0:384], ALU.subtract), t, wf[i])
                zf[i] = s
                bank_read[b] = [s]
                s = pool(lambda e: e.tensor_tensor(diag(ww), diag(ww), neg2, ALU.add), s)
                return act(lambda e: e.activation(ww, ww, ACT.Exp), s)
            pvb = [None]
            done = []

            def head_c(h, ready):
                i, hv = h % NB, slice(h * 64, h * 64 + 64)
                if h % 2 == 0:
                    pvb[0] = bank()
                b, w = pvb[0]
                P = banks[b]
                o_ = slice((h % 2) * 64, (h % 2) * 64 + 64)
                ww = WW[i]

                def go(e):
                    mm(e, P[o_, 0:256], V3[:, 0, hv], ww[:, 0:256], True, False, skip_group_check=True)
                    return mm(e, P[o_, 128:256], V3[:, 1, hv], ww[:, 256:384], False, True, skip_group_check=True)
                t = pe(go, w if h % 2 == 0 else None, ready, got["v"])
                wf[i] = t
                if h % 2:
                    r = act(lambda e: e.copy(o3[:, h // 2, :], P[:, 0:256]), t)
                    bank_read[b] = [r]
                    done.append(r)
            ra, rb = {}, {}
            for i in range(18):
                if i < 16:
                    ra[i] = head_a(i)
                if 1 <= i <= 16:
                    rb[i - 1] = head_b(i - 1, ra[i - 1])
                if i >= 2:
                    head_c(i - 2, rb[i - 2])
            return down_proj(a["sb_out"], o3, done)

        rw3 = par("rw").rearrange("p (k e) -> p k e", k=8)
        sco, sel, rank, mask, gat = (small(32) for _ in range(5))
        gsc, grk = small(8), small(8)
        wsum = small(2)
        low = con("lower").rearrange("p (i j) -> p i j", i=4)

        def router(xt):
            at[0] = 0
            ple = carve(2048)
            cmp1, cmp2 = carve(128), carve(128)
            gT = carve(256)
            GG = carve(4096)
            b, w = bank()
            P = banks[b]

            def go(e):
                for t in range(2):
                    for k in range(8):
                        i = mm(e, P[:, t * 16:t * 16 + 16], XT3[:, k, t * 128:t * 128 + 128], rw3[:, k, :], k == 0,
                               k == 7)
                return i
            t = pe(go, w, xt)
            s = act(lambda e: e.activation(sco, P[:, 0:32], ACT.Sigmoid), t)
            bank_read[b] = [s]
            v4 = sel.rearrange("p (g i) -> p g i", i=4)
            sc3 = sco.rearrange("p (t e) -> p t e", t=2)
            sel3 = sel.rearrange("p (t e) -> p t e", t=2)
            s = dve(lambda e: e.tensor_tensor(sel3, sc3, par("rb").unsqueeze(1).to_broadcast([128, 2, 16]), ALU.add), s)
            m3 = mask.rearrange("p (g i) -> p g i", i=4)
            c1 = cmp1.rearrange("p (g i j) -> p g i j", i=4, j=4)
            c2 = cmp2.rearrange("p (g i j) -> p g i j", i=4, j=4)

            def ranks(v, groups, out, s):
                vj = v.unsqueeze(2).to_broadcast([128, groups, 4, 4])
                vi = v.unsqueeze(3).to_broadcast([128, groups, 4, 4])
                lw = low.unsqueeze(1).to_broadcast([128, groups, 4, 4])
                x, y = c1[:, 0:groups, :, :], c2[:, 0:groups, :, :]
                s1 = dve(lambda e: e.tensor_tensor(x, vj, vi, ALU.is_gt), s)
                s2 = dve(lambda e: e.tensor_tensor(y, vj, vi, ALU.is_equal), s)
                s3 = dve(lambda e: e.tensor_tensor(y, y, lw, ALU.mult), s2)
                s4 = dve(lambda e: e.tensor_tensor(x, x, y, ALU.add), s3)
                return dve(lambda e: e.tensor_reduce(out, x, AX, ALU.add), s4)
            s = ranks(v4, 8, rank.rearrange("p (g i) -> p g i", i=4), s)
            s = dve(lambda e: e.tensor_scalar(mask, rank, 2.0, None, ALU.is_lt), s)
            s = dve(lambda e: e.tensor_tensor(rank, mask, sel, ALU.mult), s)
            s = dve(lambda e: e.tensor_reduce(gsc, rank.rearrange("p (g i) -> p g i", i=4), AX, ALU.add), s)
            s = ranks(gsc.rearrange("p (t g) -> p t g", t=2), 2, grk.rearrange("p (t g) -> p t g", t=2), s)
            s = dve(lambda e: e.tensor_scalar(grk, grk, 1.0, None, ALU.is_lt), s)
            s = dve(lambda e: e.tensor_tensor(m3, m3, grk.unsqueeze(2).to_broadcast([128, 8, 4]), ALU.mult), s)
            s = dve(lambda e: e.tensor_tensor(gat, mask, sco, ALU.mult), s)
            g3 = gat.rearrange("p (t e) -> p t e", t=2)
            s = dve(lambda e: e.tensor_reduce(wsum, g3, AX, ALU.add), s)
            s = dve(lambda e: e.reciprocal(wsum, wsum), s)
            s = dve(lambda e: e.tensor_tensor(g3, g3, wsum.unsqueeze(2).to_broadcast([128, 2, 16]), ALU.mult), s)
            b, w = bank()
            P = banks[b]

            def go(e):
                for t in range(2):
                    i = e.transpose(P[0:16, t * 128:t * 128 + 128], g3[:, t, :], ident)
                return i
            t = pe(go, w, s)
            gt_done = dve(lambda e: e.tensor_copy(gT[0:16, :], P[0:16, 0:256]), t)
            bank_read[b] = [gt_done]
            ready = []
            for ep in range(8):
                b, w = bank()
                P = banks[b]

                def go(e, ep=ep, P=P):
                    for k in range(2):
                        x = 2 * ep + k
                        i = mm(e, P[:, k * 256:k * 256 + 256], ident[0:16, x:x + 1].to_broadcast([16, 128]),
                               gT[0:16, :], True, True)
                    return i
                t = pe(go, w, gt_done)
                r = act(lambda e, ep=ep, P=P: e.copy(GG[:, 512 * ep:512 * ep + 512], P[:, :]), t)
                bank_read[b] = [r]
                ready.append(r)
            return ple, lambda x: (GG[:, 256 * x:256 * x + 256], ready[x // 2])

        def ple_term(i, ple, xt):
            d1 = down_proj(a["ple_gate"][i], XT3, xt, 0)
            bp = Block(a["p"][i])
            p3 = bp.view(k=2)
            d2 = down_proj(a["ple_proj"][i], p3, [bp.here], 4, 2)
            bp.done(d2)
            out = []
            for b in range(4):
                dst = ple[:, b * 512:b * 512 + 512]
                s = act(lambda e, b=b, dst=dst: e.activation(dst, banks[b][:, :], ACT.Sigmoid), d1)
                bank_read[b] = [s]
                m = dve(lambda e, b=b, dst=dst: e.tensor_tensor(dst, dst, banks[4 + b][:, :], ALU.mult), s, d2)
                bank_read[4 + b] = [m]
                x = X3[:, b // 2, (b % 2) * 512:(b % 2) * 512 + 512]
                out.append(dve(lambda e, x=x, dst=dst: e.scalar_tensor_tensor(x, x, ALPHA, dst, ALU.mult, ALU.add), m))
            return out

        xt_last = xt_read
        for i in range(2):
            xt = transposes(X3, x_ready, None, xt_last)
            d = state_space(xt, None) if i == 0 else stick_breaking(xt)
            x_ready = add_acc(ALPHA, None, d, xt)
            x_ready = layer_norm(2 * i, x_ready)
            xt = transposes(X3, x_ready, None, d)
            ple, gates = router(xt)
            ple_term(i, ple, xt)
            d, xt_last = ffn(a["moe_w13"][i], a["moe_w2"][i], 32, xt, gates)
            x_ready = add_acc(None, 1.0, d)
            x_ready = layer_norm(2 * i + 1, x_ready)
        s_out = sem("d_out")
        fin = Q.dma("sp", lambda e: e.dma_start(a["out"], X3), s_out, 16, x_ready)

        Q.number(sems)
        block = ctx.enter_context(nc.Block())

        @block.sync
        def _(e):
            Q.emit("sp", e)
            e.wait_ge(s_out, 16)

        @block.tensor
        def _(e):
            Q.emit("pe", e)

        @block.scalar
        def _(e):
            Q.emit("act", e)

        @block.vector
        def _(e):
            Q.emit("dve", e)

        @block.gpsimd
        def _(e):
            Q.emit("pool", e)


def _constants():
    f = np.float32
    c = {}
    i, j = np.arange(128)[:, None], np.arange(128)[None, :]
    c["ident"] = np.eye(128, dtype=f)
    c["ones"] = np.ones((128, 128), f)
    c["tri"] = (i >= j).astype(f)
    c["strict"] = (i < j).astype(f)
    c["neg"] = np.where(i < j, 0.0, -1e30).astype(f)

    def bias(dist):
        n = ((dist >= 0) & (dist <= 128)).astype(int) + ((dist >= 0) & (dist % 4 == 0)) + ((dist >= 0) & (dist % 16 == 0))
        return np.where(n > 0, np.log(np.maximum(n, 1)), -1e30).astype(f)
    c["abias"] = np.concatenate([bias(i - j), bias(128 + i - j), bias(i - j)], axis=1)
    c["hgm"] = ((i <= j) & (i // 64 == j // 64)).astype(f)
    c["seg"] = np.broadcast_to((np.arange(256) % 64 != 0).astype(f), (128, 256))
    inv = f(500000.0) ** (-np.arange(0, 16, 2, dtype=f) / f(16))
    ang = (np.arange(256, dtype=f)[:, None] * inv[None, :]).astype(f)
    c["cos"] = np.cos(ang).astype(f).reshape(2, 128, 8).transpose(1, 0, 2).reshape(128, 16)
    c["sin"] = np.sin(ang).astype(f).reshape(2, 128, 8).transpose(1, 0, 2).reshape(128, 16)
    w = np.array([2, 4, 8, 16])[:, None]
    c["invc"] = np.broadcast_to((1.0 / np.minimum(np.arange(16)[None, :] + 1, w)).astype(f).reshape(1, 64), (128, 64))
    k = np.arange(4)
    c["lower"] = np.broadcast_to((k[None, :] < k[:, None]).astype(f).reshape(1, 16), (128, 16))
    return np.concatenate([np.asarray(c[n], f).reshape(128, w_) for n, w_ in CONSTS], axis=1)


def _layout(inp):
    x = {k: np.asarray(v) for k, v in inp.items()}

    def colpart(v, k):
        return v.reshape(k, 128).T

    def cols(w, n):
        K, N = w.shape
        return w.reshape(K // 128, 128, N // n, n).transpose(2, 1, 0, 3).reshape(N // n, 128, K // 128 * n)

    def rows(w, k):
        K, N = w.shape
        return w.reshape(K // 128 // k, k, 128, N).transpose(0, 2, 1, 3).reshape(K // 128 // k, 128, k * N)

    def ffn(w1, w3):
        return np.stack([cols(w1, 256), cols(w3, 256)], axis=1)

    o = {}
    p = {"n1": colpart(x["ffn1_norm"], 8), "nm": colpart(x["mix_norm"], 8), "n2": colpart(x["ffn2_norm"], 8),
         "lb": x["hg_lb_logits"].reshape(2, 4, 128).transpose(2, 0, 1).reshape(128, 8),
         "hgn": x["hg_out_norm"].reshape(128, 1),
         "qn": np.broadcast_to(x["q_norm"].reshape(1, 64), (128, 64)),
         "kn": np.broadcast_to(x["k_norm"].reshape(1, 64), (128, 64)),
         "lre": x["s5_lambda_re_2"].reshape(16, 128).T, "lim": x["s5_lambda_im_2"].reshape(16, 128).T,
         "ldt": np.repeat(x["s5_log_dt_2"].reshape(16, 2), 64, axis=1).T,
         "sd": x["s5_d_2"].reshape(4, 128).T, "ps": x["pool_scale_2"].reshape(4, 128).T,
         "rb": np.broadcast_to(x["router_bias_2"].reshape(1, 16), (128, 16)),
         "rw": x["router_w_2"].reshape(8, 128, 16).transpose(1, 0, 2).reshape(128, 128)}
    for n, key in (("bre", "s5_b_re_2"), ("bim", "s5_b_im_2")):
        b = x[key].reshape(4, 4, 2, 64, 16)
        z = np.zeros((4, 2, 16, 4, 2, 64), b.dtype)
        for g in range(2):
            z[:, g, :, :, g, :] = b[:, :, g].transpose(1, 3, 0, 2)
        p[n] = z.reshape(128, 512)
    o["params"] = np.concatenate([p[n].reshape(128, w) for n, w in PARAMS], axis=1)
    cc = []
    for key in ("s5_c_re_2", "s5_c_im_2"):
        c = x[key].reshape(16, 2, 16, 64)
        z = np.zeros((2, 64, 16, 2, 16), c.dtype)
        for g in range(2):
            z[g, :, :, g, :] = c[:, g].transpose(2, 0, 1)
        cc.append(z.reshape(128, 512))
    o["s5c"] = np.concatenate(cc, axis=1)
    o["consts"] = _constants()
    o["x"] = x["x"].reshape(2, 128, 1024).transpose(1, 0, 2)
    for n in ("ffn1", "ffn2"):
        o[n + "_w13"] = ffn(x[n + "_w1"][0], x[n + "_w3"][0])
        o[n + "_w2"] = rows(x[n + "_w2"][0], 2)
    w = x["w_in"][0]
    o["w_hq"], o["w_hf"] = cols(w[:, 1536:2048], 256), cols(w[:, 2048:2560], 256)
    o["w_tok"] = np.stack([rows(w[:, s:s + 512], 4) for s in (0, 512, 1024, 2560, 3072)])
    o["w_out"] = rows(x["w_out"][0], 2)
    o["ab_in"] = cols(x["ab_w_in_2"][0], 256)
    o["pool_w"] = x["pool_w_2"][0].transpose(1, 0, 2).reshape(128, 512)
    o["w_glu"] = rows(x["s5_w_glu_2"][0], 4)[0]
    o["ab_out"] = rows(x["ab_w_out_2"][0], 2)
    w = x["sb_w_qkv_2"][0]
    o["sb_q"], o["sb_k"] = cols(w[:, 0:1024], 256), cols(w[:, 1024:2048], 256)
    o["sb_v"] = np.stack([rows(w[:, s:s + 512], 4) for s in (2048, 2560)])
    o["sb_out"] = rows(x["sb_w_out_2"][0], 2)
    o["ln_g"] = np.stack([x["ln_mix_g_2"], x["ln_ffn_g_2"]], axis=1).reshape(4, 1024)
    o["ln_b"] = np.stack([x["ln_mix_b_2"], x["ln_ffn_b_2"]], axis=1).reshape(4, 1024)
    o["p"] = x["p_2"].reshape(2, 256, 2, 128).transpose(0, 3, 2, 1).reshape(2, 128, 512)
    o["ple_proj"] = np.stack([rows(x["ple_w_proj_2"][i], 2) for i in range(2)])
    o["ple_gate"] = np.stack([rows(x["ple_w_gate_2"][i], 2) for i in range(2)])
    o["moe_w13"] = np.stack([np.concatenate([ffn(x["moe_w1_2"][i, e], x["moe_w3_2"][i, e]) for e in range(16)])
                             for i in range(2)])
    o["moe_w2"] = np.stack([np.concatenate([rows(x["moe_w2_2"][i, e], 2) for e in range(16)]) for i in range(2)])
    return {k: np.ascontiguousarray(v) for k, v in o.items()}


def kernel(**inputs):
    import concourse.bacc as _bacc
    from concourse.bass_utils import run_bass_kernel_spmd as _run

    nc = _bacc.Bacc("TRN2", target_bir_lowering=False, num_devices=1)
    arrays, args = {}, {}
    for name, v in _layout(inputs).items():
        arrays[f"in_{name}"] = v
        args[name] = nc.dram_tensor(f"in_{name}", v.shape, mybir.dt.from_np(v.dtype), kind="ExternalInput").ap()
    args["out"] = nc.dram_tensor("out_0", (2, 128, 1024), F32, kind="ExternalOutput").ap().rearrange("t p d -> p t d")
    build(nc, args)
    r = _run(nc, [arrays], core_ids=[0])
    return r.results[0]["out_0"].reshape(1, 256, 1024)
```

```python
from contextlib import ExitStack
import math

import numpy as np
import concourse.bass as bass
from concourse import mybir
from concourse.alu_op_type import AluOpType as ALU

F32 = mybir.dt.float32
I32 = mybir.dt.int32
F32R = mybir.dt.float32r
ACT = mybir.ActivationFunctionType
AX = mybir.AxisListType.X

T = 256
D = 1024
ALPHA = 4 ** 0.25
CAP = 64
RAW = 4
SPLIT = 4
AHEAD = 3
DVE_COLS = 1408
SCOLS = 2048
TWO_PI = 2 * math.pi
MAGIC = 1.5 * 2.0 ** 23

PARAMS = [("n1", 8), ("nm", 8), ("n2", 8), ("lb", 8), ("hgn", 1), ("qn", 64), ("kn", 64), ("lre", 16),
          ("lim", 16), ("ldt", 16), ("sd", 4), ("ps", 4), ("rb", 16), ("rw", 128), ("bre", 512), ("bim", 512)]
CONSTS = [("ident", 128), ("ones", 128), ("tri", 128), ("strict", 128), ("neg", 128), ("abias", 384),
          ("hgm", 128), ("seg", 256), ("cos", 16), ("sin", 16), ("invc", 64), ("lower", 16), ("iota", 64)]


def offsets(table):
    at, out = 0, {}
    for name, n in table:
        out[name] = (at, n)
        at += n
    return out, at


class Op:

    def __init__(self, eng, fn, after):
        self.eng, self.fn, self.after = eng, fn, after
        self.wanted = False
        self.sem, self.value, self.by = None, None, 1


class Arms:

    def __init__(self, flag, limit, ready):
        self.flag, self.limit, self.ready = flag, limit, ready
        self.arms = ({}, {})
        self.ends = {}
        self.pads = {}


class Queues:

    ENGINES = ("pe", "act", "dve", "pool")

    def __init__(self):
        self.main = {e: [] for e in self.ENGINES + ("sp",)}
        self.q = self.main

    def put(self, eng, fn, *after):
        flat = []

        def add(x):
            if isinstance(x, (list, tuple)):
                for y in x:
                    add(y)
            elif x is not None:
                x.wanted = True
                flat.append(x)
        add(after)
        op = Op(eng, fn, flat)
        (self.main if eng == "sp" else self.q)[eng].append(op)
        return op

    def fixed(self, op, sem, value, by=1):
        op.sem, op.value, op.by = sem, value, by
        return op

    def split(self, flag, limit, ready):
        r = Arms(flag, limit, ready)
        ready.wanted = True
        for e in self.ENGINES:
            self.main[e].append(r)
        return r

    def enter(self, arms, which):
        self.q = arms.arms[which]
        for e in self.ENGINES:
            self.q.setdefault(e, [])

    def leave(self, arms):
        self.q = self.main
        for arm in arms.arms:
            for e in self.ENGINES:
                own = [o for o in arm[e] if o.sem is None]
                if own:
                    own[-1].wanted = True
        arms.ends = {e: Op(e, None, []) for e in self.ENGINES}
        return arms.ends

    def number(self, sems):
        for eng, ops in self.main.items():
            n = 0

            def count(ops, n):
                for op in ops:
                    if op.sem is None and op.wanted:
                        n += 1
                        op.sem, op.value = sems[eng], n
                return n
            for op in ops:
                if isinstance(op, Arms):
                    each = [count(arm[eng], n) for arm in op.arms]
                    n = max(each)
                    op.pads[eng] = [(sems[eng], m, n - m) for m in each]
                    op.ends[eng].sem, op.ends[eng].value = sems[eng], n
                else:
                    n = count([op], n)

    def emit(self, eng, handle):
        def wait(after, seen):
            need = {}
            for a in after:
                if need.get(a.sem.name, (None, 0))[1] < a.value:
                    need[a.sem.name] = (a.sem, a.value)
            for name, (sem, v) in need.items():
                if seen.get(name, 0) < v:
                    handle.wait_ge(sem, v)
                    seen[name] = v

        def run(ops, seen):
            for op in ops:
                if isinstance(op, Arms):
                    wait([op.ready], seen)
                    v = handle.value_load(op.flag, min_val=0, max_val=T)
                    with handle.If(v < op.limit):
                        arm(op, 0, dict(seen))
                    with handle.Else():
                        arm(op, 1, dict(seen))
                    continue
                wait(op.after, seen)
                ins = op.fn(handle)
                if op.sem is not None:
                    ins.then_inc(op.sem, op.by)

        def arm(op, which, seen):
            run(op.arms[which][eng], seen)
            sem, at, pad = op.pads[eng][which]
            if pad:
                handle.wait_ge(sem, at)
                handle.sem_inc(sem, pad)
        run(self.main[eng], {})


def build(nc, a):
    Q = Queues()
    ctx = ExitStack()
    with ctx:
        base = -(-nc.sbuf_base // 64) * 64
        mem = [0]

        def place(name, at, cols, dt=F32):
            return nc.alloc_sbuf_tensor_at(name, [128, cols], dt, offset=base + 4 * at)[:, :]

        def sb(name, cols, dt=F32):
            at = mem[0]
            mem[0] += -(-cols // 16) * 16
            return place(name, at, cols, dt)

        def sem(name):
            return ctx.enter_context(nc.semaphore(name))

        raw = sb("raw", RAW * SCOLS)
        whi, wlo = sb("whi", SPLIT * SCOLS, F32R), sb("wlo", SPLIT * SCOLS, F32R)
        Xs = sb("Xs", 2048)
        XN = sb("XN", 2048)
        XNr = place("XNr", mem[0] - 2048, 2048, F32R)
        xt_at = mem[0]
        XTh, XTl = sb("XTh", 2048, F32R), sb("XTl", 2048, F32R)
        po, pn = offsets(PARAMS)
        co, cn = offsets(CONSTS)
        PR = sb("PR", pn)
        CO = sb("CO", cn)
        SM = sb("SM", 640)
        flag = sb("flag", 16, I32)[:, 0:1]
        rwh, rwl = sb("rwh", 128, F32R), sb("rwl", 128, F32R)
        identr, twin = sb("identr", 128, F32R), sb("twin", 128)
        ident2 = twin[:, 0:64]
        gsplit = sb("gsplit", 64, F32R)
        rest = mem[0]
        rest_cols = (nc.sbuf_usable_end - base) // 4 - rest
        FB = 9728
        CS, CM = place("CS", rest, 8192), place("CM", rest + 8192, 1536)
        HS, HF = place("HS", rest + FB, 1024), place("HF", rest + FB + 1024, 1024)
        HTh, HTl = place("HTh", rest + FB + 2048, 1024, F32R), place("HTl", rest + FB + 3072, 1024, F32R)
        TMP = place("TMP", rest + FB + 4096, 2048)
        n_phase = [0]

        def phase(start=0):
            n_phase[0] += 1
            at, tag = [start], f"p{n_phase[0]}_"

            def carve(cols, dt=F32):
                at[0] += cols
                assert at[0] <= rest_cols, (at, rest_cols)
                return place(f"{tag}{at[0]}", rest + at[0] - cols, cols, dt)
            carve.at = at
            return carve

        banks = [ctx.enter_context(nc.psum_tensor(f"pb{i}", [128, 512], F32)) for i in range(8)]
        sems = {e: sem("e_" + e) for e in Q.ENGINES}
        raw_sem = [sem(f"raw{i}") for i in range(RAW)]
        hi_sem = [sem(f"hi{i}") for i in range(SPLIT)]
        lo_sem = [sem(f"lo{i}") for i in range(SPLIT)]
        used_sem = [sem(f"used{i}") for i in range(SPLIT)]

        def par(name, lo=0, n=None):
            o, w = po[name]
            return PR[:, o + lo:o + lo + (w - lo if n is None else n)]

        def con(name, lo=0, n=None):
            o, w = co[name]
            return CO[:, o + lo:o + lo + (w - lo if n is None else n)]

        ident = con("ident")
        X3 = Xs[:, :].rearrange("p (t d) -> p t d", t=2)
        XN3 = XN[:, :].rearrange("p (t d) -> p t d", t=2)
        XT3 = [x.rearrange("p (k t) -> p k t", k=8) for x in (XTh, XTl)]

        small_at = [0]

        def small(n):
            at = small_at[0]
            small_at[0] += n
            assert small_at[0] <= 640
            return SM[:, at:at + n]

        def pe(fn, *after):
            return Q.put("pe", fn, *after)

        def act(fn, *after):
            return Q.put("act", fn, *after)

        def dve(fn, *after):
            return Q.put("dve", fn, *after)

        def pool(fn, *after):
            return Q.put("pool", fn, *after)

        n_misc = [0]

        def load(dst, src, *after, eng="act"):
            n_misc[0] += 1
            return Q.fixed(Q.put(eng, lambda e: e.dma_start(dst, src), *after), sem(f"d_m{n_misc[0]}"), 16, 16)

        plan = []
        state = {"split": 0, "use": 0}
        split_done, used = {}, {}
        ahead = [SPLIT]
        shared = set()

        def plan_ffn(w13, w2, groups, lag=1):
            for g in range(groups):
                plan.extend([w13[2 * g], w13[2 * g + 1]])
                if g >= lag:
                    plan.append(w2[g - lag])
            for g in range(groups - lag, groups):
                plan.append(w2[g])

        def plan_all(*srcs):
            for x in srcs:
                plan.extend(x[i] for i in range(x.shape[0]))

        def queue_loads():
            for n, src in enumerate(plan):
                dst = raw[:, n % RAW * SCOLS:n % RAW * SCOLS + src.shape[-1]]
                free = Op("dve", None, [])
                if n >= RAW:
                    m = n - RAW
                    Q.fixed(free, lo_sem[m % SPLIT], 2 * (m // SPLIT + 1))
                op = Q.put("sp", lambda e, dst=dst, src=src: e.dma_start(dst, src), free if n >= RAW else None)
                Q.fixed(op, raw_sem[n % RAW], 16 * (n // RAW + 1), 16)
                loaded.append(op)

        loaded = []

        def split_block():
            n = state["split"]
            state["split"] += 1
            cols, s, r = plan[n].shape[-1], n % SPLIT * SCOLS, n % RAW * SCOLS
            x, h, l = raw[:, r:r + cols], whi[:, s:s + cols], wlo[:, s:s + cols]
            c = act(lambda e: e.copy(h, x), loaded[n], used.get(n - SPLIT))
            Q.fixed(c, hi_sem[n % SPLIT], n // SPLIT + 1)
            cut = DVE_COLS if n in shared else cols
            split_done[n] = []
            for eng, lo, hi in ((dve, 0, cut), (pool, cut, cols)):
                if lo < hi:
                    o = eng(lambda e, f=slice(lo, hi): e.tensor_tensor(l[:, f], x[:, f], h[:, f].bitcast(F32),
                                                                       ALU.subtract), c)
                    split_done[n].append(Q.fixed(o, lo_sem[n % SPLIT], 2 * (n // SPLIT + 1), 2 if cut == cols else 1))

        def pump(more=0):
            while state["split"] < min(len(plan), state["use"] + ahead[0] + more) and (
                    state["split"] < SPLIT or state["split"] - SPLIT in used):
                split_block()

        class Block:

            def __init__(self, src):
                self.n = state["use"]
                state["use"] += 1
                assert plan[self.n].tensor.name == src.tensor.name and plan[self.n].offset == src.offset
                pump()
                assert self.n < state["split"]
                s, cols = self.n % SPLIT * SCOLS, src.shape[-1]
                self.ap = whi[:, s:s + cols], wlo[:, s:s + cols]
                self.here = split_done[self.n]

            def done(self, op):
                used[self.n] = Q.fixed(op, used_sem[self.n % SPLIT], self.n // SPLIT + 1)

            def view(self, **kw):
                (k, v), = kw.items()
                return [x.rearrange(f"p ({k} n) -> p {k} n", **{k: v}) for x in self.ap]

        bank_read = [[] for _ in range(8)]
        turn, held = [0], set()

        def bank(first=0):
            turn[0] += 1
            b = first + turn[0] % (8 - first)
            if b in held:
                return bank(first)
            w = bank_read[b]
            bank_read[b] = []
            return b, w

        def mm(e, out, l, r, start, stop, **kw):
            return e.matmul(out, l, r, start=start, stop=stop, **kw)

        def mm3(e, out, l, r, start, stop):
            mm(e, out, l[0], r[0], start, False)
            mm(e, out, l[0], r[1], False, False)
            return mm(e, out, l[1], r[0], False, stop)

        def both(x, f):
            return [f(y) for y in x]

        def split2(dst, src, ready, free=None, scale=None):
            h, l = dst
            if scale is None:
                c = act(lambda e: e.copy(h, src), ready, free)
                return dve(lambda e: e.tensor_tensor(l, src, h.bitcast(F32), ALU.subtract), c)
            c = act(lambda e: e.activation(h, src, ACT.Copy, scale=scale), ready, free)
            return dve(lambda e: e.scalar_tensor_tensor(l, src, scale, h.bitcast(F32), ALU.mult, ALU.subtract), c)

        l_x = load(X3, a["x"], eng="sp")
        l_con = load(CO[:, :], a["consts"], eng="sp")
        l_par = load(PR[:, :], a["params"], eng="sp")

        rs = small(2)
        ss = small(2)

        def transposes(src3, src_ready, weight, xt_read):
            out = []
            for kp in range(4):
                b, w = bank()
                P = banks[b]

                def go(e, kp=kp, P=P):
                    for k in range(2):
                        for t in range(2):
                            i = e.transpose(P[:, k * 256 + t * 128:k * 256 + t * 128 + 128],
                                            src3[:, t, (2 * kp + k) * 128:(2 * kp + k + 1) * 128], ident)
                    return i
                t = pe(go, w, src_ready, l_con)
                if weight is None:
                    r = split2([x[:, kp * 512:kp * 512 + 512] for x in (XTh, XTl)], P[:, :], t, xt_read)
                else:
                    for k in range(2):
                        i = 2 * kp + k
                        r = split2(both(XT3, lambda x: x[:, i, :]), P[:, k * 256:k * 256 + 256], [t, r] if k else [t, l_par],
                                   xt_read, weight[:, i:i + 1])
                out.append(r)
                bank_read[b] = [r]
            pump()
            return out

        def rms_transpose(x_ready, weight, xn_free, xt_read):
            ready = []
            for t in range(2):
                s1 = dve(lambda e, t=t: e.tensor_tensor_reduce(XN3[:, t, :], X3[:, t, :], X3[:, t, :], 1.0, 0.0,
                                                               ALU.mult, ALU.add, ss[:, t:t + 1]), x_ready, xn_free)
            s2 = dve(lambda e: e.tensor_scalar(rs, ss, 1.0 / D, 1e-6, ALU.mult, ALU.add), s1)
            s3 = act(lambda e: e.activation(rs, rs, ACT.Sqrt), s2)
            s4 = dve(lambda e: e.reciprocal(rs, rs), s3)
            for t in range(2):
                ready.append(dve(lambda e, t=t: e.tensor_scalar(XN3[:, t, :], X3[:, t, :], rs[:, t:t + 1], None,
                                                                ALU.mult), s4))
            return transposes(XN3, ready, weight, xt_read)

        hs_read, hf_read = [None] * 4, [None] * 4

        def ffn(w13, w2, groups, xt_ready, gates=None, lag=1, HT=(HTh, HTl), first_read=None):
            acc_free = [x for b in range(4) for x in bank_read[b]]
            total = 2 * groups
            slots = 2 * lag + 2
            hTs = both(HT, lambda x: x.rearrange("p (s t) -> p s t", s=slots))
            ht_read = [first_read] * slots
            ready = {}

            def down(g):
                blk = Block(w2[g])
                W = blk.view(c=2)

                def go(e):
                    for c in range(2):
                        n = 2 * g + c
                        for t in range(2):
                            for h in range(2):
                                i = mm3(e, banks[2 * t + h][:, :],
                                        both(hTs, lambda x: x[:, n % slots, t * 128:t * 128 + 128]),
                                        both(W, lambda x: x[:, c, h * 512:h * 512 + 512]), n == 0, n == total - 1)
                    return i
                d = pe(go, ready[2 * g], ready[2 * g + 1], blk.here, acc_free if g == 0 else None)
                blk.done(d)
                ht_read[2 * g % slots] = ht_read[(2 * g + 1) % slots] = d
                return d

            for g in range(groups):
                for c in range(2):
                    n = 2 * g + c
                    blk = Block(w13[n])
                    b, w = bank(4)
                    P = banks[b]

                    def up(e, W=both(blk.ap, lambda x: x.rearrange("p (k c f) -> p k c f", k=8, c=2)), P=P):
                        for half in range(2):
                            for k in range(8):
                                i = mm3(e, P[:, half * 256:half * 256 + 256], both(W, lambda x: x[:, k, half, :]),
                                        both(XT3, lambda x: x[:, k, :]), k == 0, k == 7)
                        return i
                    u = pe(up, w, blk.here, xt_ready)
                    blk.done(u)
                    s = n % 4
                    hs, hf = HS[:, s * 256:s * 256 + 256], HF[:, s * 256:s * 256 + 256]
                    sl = act(lambda e, hs=hs, P=P: e.activation(hs, P[:, 0:256], ACT.Silu), u, hs_read[s])
                    if gates is not None:
                        gate, g_ready = gates(g // 2)
                        sl = pool(lambda e, hs=hs, gate=gate: e.tensor_tensor(hs, hs, gate, ALU.mult), sl, g_ready)
                    m = dve(lambda e, hs=hs, hf=hf, P=P: e.tensor_tensor(hf, hs, P[:, 256:512], ALU.mult),
                            sl, hf_read[s])
                    hs_read[s] = m
                    bank_read[b] = [m]
                    ready[n] = hf_read[s] = split2(both(hTs, lambda x: x[:, n % slots, :]), hf, m, ht_read[n % slots])
                    pump()
                if g >= lag:
                    down(g - lag)
                    pump()
            for g in range(groups - lag, groups):
                d = down(g)
            return d

        def add_acc(scale_x, scale_acc, ready, x_ready=None):
            out = []
            for b in range(4):
                x = X3[:, b // 2, (b % 2) * 512:(b % 2) * 512 + 512]
                if scale_x is None:
                    o = dve(lambda e, x=x, b=b: e.scalar_tensor_tensor(x, banks[b][:, :], scale_acc, x, ALU.mult,
                                                                       ALU.add), ready, x_ready)
                else:
                    o = dve(lambda e, x=x, b=b: e.scalar_tensor_tensor(x, x, scale_x, banks[b][:, :], ALU.mult,
                                                                       ALU.add), ready, x_ready)
                bank_read[b] = [o]
                out.append(o)
            return out

        def down_proj(src, lhs3, ready, first=0, kcount=8, between=None):
            free = [x for b in range(first, first + 4) for x in bank_read[b]]
            for g in range(kcount // 2):
                blk = Block(src[g])

                def go(e, g=g, W=blk.view(c=2)):
                    for c in range(2):
                        k = 2 * g + c
                        for t in range(2):
                            for h in range(2):
                                i = mm3(e, banks[first + 2 * t + h][:, :],
                                        both(lhs3, lambda x: x[:, k, t * 128:t * 128 + 128]),
                                        both(W, lambda x: x[:, c, h * 512:h * 512 + 512]), k == 0, k == kcount - 1)
                    return i
                d = pe(go, blk.here, ready[g] if isinstance(ready, dict) else ready if g == 0 else None,
                       free if g == 0 else None)
                blk.done(d)
                if g < kcount // 2 - 1:
                    pump()
                if between and g in between:
                    between[g]()
            return d

        def proj_T(src, rhs3, ready, evac, kcount=8):
            for g in range(src.shape[0]):
                blk = Block(src[g])
                b, w = bank()
                P = banks[b]

                def go(e, W=blk.view(k=kcount), P=P):
                    for c in range(2):
                        for k in range(kcount):
                            i = mm3(e, P[:, c * 256:c * 256 + 256], both(W, lambda x: x[:, k, c * 128:c * 128 + 128]),
                                    both(rhs3, lambda x: x[:, k, :]), k == 0, k == kcount - 1)
                    return i
                d = pe(go, blk.here, w, ready if g == 0 else None)
                blk.done(d)
                bank_read[b] = evac(g, P, d)
                pump()
            return d

        def proj_tok(src, ready, evac):
            b0, w0 = bank()
            b1, w1 = bank()
            ds = [None, None]
            for half in range(2):
                blk = Block(src[half])
                W = blk.view(k=4)
                for t, b in ((0, b0), (1, b1)):
                    def go(e, half=half, t=t, b=b, W=W):
                        for k in range(4):
                            i = mm3(e, banks[b][:, :], both(XT3, lambda x: x[:, 4 * half + k, t * 128:t * 128 + 128]),
                                    both(W, lambda x: x[:, k, :]), half == 0 and k == 0, half == 1 and k == 3)
                        return i
                    ds[t] = pe(go, blk.here, (w0, w1)[t] if half == 0 else None, ready)
                blk.done(ds[1])
                if half == 0:
                    pump()
            for t, b in ((0, b0), (1, b1)):
                bank_read[b] = evac(t, banks[b], ds[t])
            return ds[1]

        mag = small(16)
        CS4 = CS.rearrange("p (j c t) -> p j c t", j=16, c=2)
        CM3 = [CM[:, 512 * i:512 * i + 512].rearrange("p (j h) -> p j h", j=16) for i in range(3)]

        def tables(free):
            lre, lim, ldt = par("lre"), par("lim"), par("ldt")
            dt_, ang, kk, rr, sn, sh, cs, den, t1, t2, t3, t4, fre, fim = (small(16) for _ in range(14))
            cn, sn2 = small(16), small(16)
            o = act(lambda e: e.activation(dt_, ldt, ACT.Exp), l_par, free)
            o = dve(lambda e: e.tensor_tensor(t1, lre, dt_, ALU.mult), o)
            o_mag = act(lambda e: e.activation(mag, t1, ACT.Exp), o)
            o = dve(lambda e: e.tensor_tensor(ang, lim, dt_, ALU.mult), o)
            o = dve(lambda e: e.tensor_scalar(kk, ang, 1.0 / TWO_PI, MAGIC, ALU.mult, ALU.add), o)
            o = dve(lambda e: e.tensor_scalar(kk, kk, MAGIC, None, ALU.subtract), o)
            o = dve(lambda e: e.scalar_tensor_tensor(rr, kk, -6.28125, ang, ALU.mult, ALU.add), o)
            o = dve(lambda e: e.scalar_tensor_tensor(rr, kk, -(TWO_PI - 6.28125), rr, ALU.mult, ALU.add), o)
            o = dve(lambda e: e.tensor_scalar(rr, rr, -3.1415925, 3.1415925, ALU.max, ALU.min), o)
            o1 = act(lambda e: e.activation(sn, rr, ACT.Sin), o)
            o2 = act(lambda e: e.activation(sh, rr, ACT.Sin, scale=0.5), o)
            o = dve(lambda e: e.tensor_tensor(cs, sh, sh, ALU.mult), o2)
            o_e1 = dve(lambda e: e.tensor_scalar(cs, cs, -2.0, 1.0, ALU.mult, ALU.add), o)
            o = dve(lambda e: e.tensor_tensor(t1, mag, cs, ALU.mult), o_e1, o_mag)
            o = dve(lambda e: e.tensor_scalar(t1, t1, -1.0, None, ALU.add), o)
            o = dve(lambda e: e.tensor_tensor(t2, mag, sn, ALU.mult), o, o1)
            o = dve(lambda e: e.tensor_tensor(den, lre, lre, ALU.mult))
            o = dve(lambda e: e.tensor_tensor(t3, lim, lim, ALU.mult))
            o = dve(lambda e: e.tensor_tensor(den, den, t3, ALU.add), o)
            o = dve(lambda e: e.reciprocal(den, den), o)
            o = dve(lambda e: e.tensor_tensor(fre, t1, lre, ALU.mult), o)
            o = dve(lambda e: e.tensor_tensor(t3, t2, lim, ALU.mult), o)
            o = dve(lambda e: e.tensor_tensor(fre, fre, t3, ALU.add), o)
            o = dve(lambda e: e.tensor_tensor(fre, fre, den, ALU.mult), o)
            o = dve(lambda e: e.tensor_tensor(fim, t2, lre, ALU.mult), o)
            o = dve(lambda e: e.tensor_tensor(t3, t1, lim, ALU.mult), o)
            o = dve(lambda e: e.tensor_tensor(fim, fim, t3, ALU.subtract), o)
            o_f = dve(lambda e: e.tensor_tensor(fim, fim, den, ALU.mult), o)
            craw = [CM3[0], CM3[1]]
            l_c = load(CM[:, 0:1024], a["s5c"], free)
            ctmp, ctm2 = (TMP[:, 512 * i:512 * i + 512].rearrange("p (j h) -> p j h", j=16) for i in range(2))

            def bc(x, n):
                return x.unsqueeze(2).to_broadcast([128, 16, n])
            o = pool(lambda e: e.tensor_tensor(ctmp, craw[0], bc(fre, 32), ALU.mult), o_f, l_c, free)
            o = pool(lambda e: e.tensor_tensor(ctm2, craw[1], bc(fim, 32), ALU.mult))
            o = pool(lambda e: e.tensor_tensor(CM3[2], craw[0], bc(fim, 32), ALU.mult), o)
            o = pool(lambda e: e.tensor_tensor(CM3[0], ctmp, ctm2, ALU.subtract), o)
            o = pool(lambda e: e.tensor_tensor(ctmp, craw[1], bc(fre, 32), ALU.mult), o)
            o = pool(lambda e: e.tensor_tensor(CM3[2], CM3[2], ctmp, ALU.add), o)
            o = pool(lambda e: e.tensor_scalar(CM3[2], CM3[2], -1.0, 0.0, ALU.mult, ALU.add), o)
            o_cm = pool(lambda e: e.tensor_scalar(CM3[1], CM3[0], -1.0, 0.0, ALU.mult, ALU.add), o)
            o = pool(lambda e: e.memset(CS4[:, :, 0, 0:1], 1.0), free)
            o = pool(lambda e: e.memset(CS4[:, :, 1, 0:1], 0.0))
            cur = [pool(lambda e: e.tensor_copy(cn, cs), o_e1), pool(lambda e: e.tensor_copy(sn2, sn), o1), o, o_cm]
            n = 1
            while n < T:
                step = min(16, 1024 // n)
                for j in range(0, 16, step):
                    J = slice(j, j + step)
                    c0, s0 = CS4[:, J, 0, 0:n], CS4[:, J, 1, 0:n]
                    c1, s1 = CS4[:, J, 0, n:2 * n], CS4[:, J, 1, n:2 * n]
                    A, B = (TMP[:, 1024 * i:1024 * i + step * n].rearrange("p (j t) -> p j t", j=step) for i in range(2))
                    cb, sb_ = (x[:, J].unsqueeze(2).to_broadcast([128, step, n]) for x in (cn, sn2))

                    def tt(out, x, y, op, *after):
                        return pool(lambda e: e.tensor_tensor(out, x, y, op), *after)
                    p = tt(A, c0, cb, ALU.mult, cur)
                    p = tt(B, s0, sb_, ALU.mult)
                    p = tt(c1, A, B, ALU.subtract, p)
                    p = tt(A, s0, cb, ALU.mult, p)
                    p = tt(B, c0, sb_, ALU.mult, p)
                    p6 = tt(s1, A, B, ALU.add, p)
                    cur = cur + [p6]
                q1 = pool(lambda e: e.tensor_tensor(t3, cn, cn, ALU.mult), o_f, p6)
                q2 = pool(lambda e: e.tensor_tensor(t4, sn2, sn2, ALU.mult), q1)
                q3 = pool(lambda e: e.tensor_tensor(sn2, sn2, cn, ALU.mult), q2)
                q4 = pool(lambda e: e.tensor_tensor(cn, t3, t4, ALU.subtract), q3)
                q5 = pool(lambda e: e.tensor_scalar(sn2, sn2, 2.0, 0.0, ALU.mult, ALU.add), q4)
                cur = [q5, p6]
                n *= 2
            return cur

        plan_ffn(a["ffn1_w13"], a["ffn1_w2"], 11)
        plan_all(a["w_hf"], a["w_hq"], *(a["w_tok"][i] for i in range(5)), a["w_out"])
        plan_ffn(a["ffn2_w13"], a["ffn2_w2"], 11)
        plan_all(a["ab_in"])
        plan.append(a["pool_w"])
        plan.append(a["w_glu"])
        plan_all(a["ab_out"])
        for i in range(2):
            if i:
                plan_all(a["sb_v"][0], a["sb_v"][1])
                for g in range(4):
                    plan.extend([a["sb_q"][g], a["sb_k"][g]])
                plan_all(a["sb_out"])
            plan_all(a["ple_gate"][i])
            plan.append(a["p"][i])
            plan_all(a["ple_proj"][i])
            first = len(plan)
            plan_ffn(a["moe_w13"][i], a["moe_w2"][i], 32, 2)
            shared.update(range(first, len(plan)))
        queue_loads()

        x_ready = [l_x]
        xt = rms_transpose(x_ready, par("n1"), None, None)

        rw_ready = split2((rwh, rwl), par("rw"), l_par)

        ident_split = act(lambda e: e.copy(identr, ident), l_con)
        id2_ready = [dve(lambda e, x=x: e.tensor_tensor(x, con("ident", 0, 64), con("ident", 64, 64), ALU.add), l_con)
                     for x in (twin[:, 0:64], twin[:, 64:128])]

        lbv = par("lb").rearrange("p (i h) -> p i h", i=2)
        lm, l0, l1, lb1, lbs = small(4), small(4), small(4), small(4), small(4)
        o = dve(lambda e: e.tensor_tensor(lm, lbv[:, 0, :], lbv[:, 1, :], ALU.max), l_par)
        o0 = dve(lambda e: e.tensor_tensor(l0, lbv[:, 0, :], lm, ALU.subtract), o)
        o1 = dve(lambda e: e.tensor_tensor(l1, lbv[:, 1, :], lm, ALU.subtract), o)
        o = act(lambda e: e.activation(l0, l0, ACT.Exp), o0)
        o = act(lambda e: e.activation(l1, l1, ACT.Exp), o1)
        o = dve(lambda e: e.tensor_tensor(l1, l0, l1, ALU.add), o)
        o = dve(lambda e: e.reciprocal(l1, l1), o)
        o = dve(lambda e: e.tensor_tensor(lbs, l0, l1, ALU.mult), o)
        lb_ready = dve(lambda e: e.tensor_scalar(lb1, lbs, -1.0, 1.0, ALU.mult, ALU.add), o)

        d = ffn(a["ffn1_w13"], a["ffn1_w2"], 11, xt)
        x_ready = add_acc(None, 0.5, d)

        xt = rms_transpose(x_ready, par("nm"), xt, None)
        carve = phase()
        F, Gt, G, E1, E2 = (carve(1024) for _ in range(5))
        qk = [carve(1024), carve(1024)]
        V, HI, SHG = carve(1024), carve(1024), carve(1024)
        qkT = [carve(1024), carve(1024)]
        attS, ksT = G, F
        prev = carve(1536)
        NP = 3
        PB = [carve(384) for _ in range(NP)]
        PT = [carve(384) for _ in range(NP)]
        rope_t = PT[NP - 1]

        f_done = []

        def evac_f(g, P, d):
            r = act(lambda e: e.activation(F[:, g * 512:g * 512 + 512], P[:, :], ACT.Sigmoid), d)
            f_done.append(r)
            return [r]
        proj_T(a["w_hf"], XT3, xt, evac_f)
        fg = []
        for h in range(4):
            fh = F[:, h * 256:h * 256 + 256]
            fg.append(dve(lambda e, fh=fh, h=h: e.tensor_scalar(fh, fh, lb1[:, h:h + 1], lbs[:, h:h + 1], ALU.mult,
                                                                ALU.add), f_done[h // 2], lb_ready))
        lg = act(lambda e: e.activation(Gt, F, ACT.Ln), fg)
        kd = dve(lambda e: e.tensor_scalar(F, F, -1.0, 1.0, ALU.mult, ALU.add), lg)
        for h in range(4):
            sl = slice(h * 256, h * 256 + 256)
            sc = dve(lambda e, sl=sl: e.tensor_tensor_scan(G[:, sl], con("seg"), Gt[:, sl], 0.0, ALU.mult, ALU.add),
                     lg, l_con)
        G16 = G.rearrange("p (c t) -> p c t", t=64)
        Gt16 = Gt.rearrange("p (c t) -> p c t", t=64)
        gl = G16[:, :, 63:64]
        df = dve(lambda e: e.tensor_tensor(Gt16, gl.to_broadcast([128, 16, 64]), G16, ALU.subtract), sc)
        e1 = act(lambda e: e.activation(E1, G, ACT.Exp), sc)
        e2 = act(lambda e: e.activation(E2, G, ACT.Exp, scale=-1.0), sc)
        dec = small(16)
        e3 = act(lambda e: e.activation(dec.unsqueeze(2), gl, ACT.Exp), sc)
        e4 = act(lambda e: e.activation(Gt, Gt, ACT.Exp), df)
        k_dec = dve(lambda e: e.tensor_tensor(E2, E2, F, ALU.mult), e2, kd)
        k_st = dve(lambda e: e.tensor_tensor(Gt, Gt, F, ALU.mult), e4)
        z_att = pool(lambda e: e.memset(attS, 0.0), e1, e2, e3, df)
        q_dec = []

        def evac_q(g, P, d):
            s = E1[:, g * 512:g * 512 + 512]
            r = dve(lambda e: e.tensor_tensor(s, s, P[:, :], ALU.mult), d, e1)
            q_dec.append(r)
            return [r]
        proj_T(a["w_hq"], XT3, None, evac_q)

        norm_w = [par("qn"), par("kn")]
        hss = [small(16), small(16)]
        att_ready = [[], []]
        cosv = con("cos").rearrange("p (t i) -> p t i", t=2)
        sinv = con("sin").rearrange("p (t i) -> p t i", t=2)
        rope_free = [None]
        for i in range(2):
            q4 = qk[i].rearrange("p (t h d) -> p t h d", t=2, h=8)
            hs3 = hss[i].rearrange("p (t h) -> p t h", t=2)

            def evac(t, P, d, i=i, q4=q4, hs3=hs3):
                Ph = P[:, :].rearrange("p (h d) -> p h d", h=8)
                sq = act(lambda e: e.activation(q4[:, t, :, :], Ph, ACT.Square), d)
                s = dve(lambda e: e.tensor_reduce(hs3[:, t, :], q4[:, t, :, :], AX, ALU.add), sq)
                s = dve(lambda e: e.tensor_scalar(hs3[:, t, :], hs3[:, t, :], 1.0 / 64, 1e-6, ALU.mult, ALU.add), s)
                s = act(lambda e: e.activation(hs3[:, t, :], hs3[:, t, :], ACT.Sqrt), s)
                s = dve(lambda e: e.reciprocal(hs3[:, t, :], hs3[:, t, :]), s)
                m = dve(lambda e: e.tensor_tensor(q4[:, t, :, :], Ph,
                                                  hs3[:, t, :].unsqueeze(2).to_broadcast([128, 8, 64]), ALU.mult), s)
                w = pool(lambda e: e.tensor_tensor(q4[:, t, :, :], q4[:, t, :, :],
                                                   norm_w[i].unsqueeze(1).to_broadcast([128, 8, 64]), ALU.mult), m)
                R = [rope_t[:, 64 * j:64 * j + 64].rearrange("p (h i) -> p h i", h=8) for j in range(4)]
                c = cosv[:, t, :].unsqueeze(1).to_broadcast([128, 8, 8])
                s_ = sinv[:, t, :].unsqueeze(1).to_broadcast([128, 8, 8])
                x1, x2 = q4[:, t, :, 0:8], q4[:, t, :, 8:16]
                r = pool(lambda e: e.tensor_tensor(R[0], x1, c, ALU.mult), w, rope_free[0])
                r = pool(lambda e: e.tensor_tensor(R[1], x2, s_, ALU.mult))
                r = pool(lambda e: e.tensor_tensor(R[2], x1, s_, ALU.mult))
                r = pool(lambda e: e.tensor_tensor(R[3], x2, c, ALU.mult))
                r = pool(lambda e: e.tensor_tensor(x1, R[0], R[1], ALU.subtract), r)
                r = pool(lambda e: e.tensor_tensor(x2, R[2], R[3], ALU.add))
                rope_free[0] = r
                att_ready[i].append(r)
                return [m]
            proj_tok(a["w_tok"][i], None, evac)

        keep = {}

        def evac_to(buf, key, func):
            keep[key] = []

            def evac(t, P, d):
                dst = buf[:, t * 512:t * 512 + 512]
                r = act(lambda e: e.activation(dst, P[:, :], func), d)
                keep[key].append(r)
                return [r]
            return evac
        proj_tok(a["w_tok"][2], None, evac_to(V, "v", ACT.Copy))
        proj_tok(a["w_tok"][3], None, evac_to(HI, "hi", ACT.Copy))
        p_last = proj_tok(a["w_tok"][4], None, evac_to(SHG, "hg", ACT.Silu))


        HI3 = HI.rearrange("p (t d) -> p t d", t=2)
        SHG3 = SHG.rearrange("p (t d) -> p t d", t=2)
        E1h = E1.rearrange("p (h t) -> p h t", h=4)
        E2h = E2.rearrange("p (h t) -> p h t", h=4)
        Kst = Gt.rearrange("p (h t) -> p h t", h=4)
        att8 = attS.rearrange("p (i t) -> p i t", i=8)
        ks8 = ksT.rearrange("p (i t) -> p i t", i=8)
        prv = prev.rearrange("p (c h v) -> p c h v", c=3, h=4)
        hgm = con("hgm").bitcast(I32)
        att_done, ks_done = [], []
        def rec_head(h):
            b, w = bank()
            P = banks[b]

            def go(e, h=h, P=P):
                for t in range(2):
                    s = slice(t * 128, t * 128 + 128)
                    mm(e, P[:, s], E2h[:, h, s], E1h[:, h, s], True, True)
                for t in range(2):
                    i = e.transpose(P[:, 256 + t * 128:384 + t * 128], Kst[:, h, t * 128:t * 128 + 128], ident)
                return i
            t = pe(go, w, q_dec, k_dec, k_st)
            rd = []
            for tt in range(2):
                rd.append(dve(lambda e, h=h, tt=tt, P=P: e.copy_predicated(
                    att8[:, 2 * h + tt, :], hgm, P[:, tt * 128:tt * 128 + 128]), t, z_att))
            att_done.append(rd[-1])
            k = act(lambda e, h=h, P=P: e.copy(ksT[:, h * 256:h * 256 + 256], P[:, 256:512]), rd[-1])
            ks_done.append(k)
            bank_read[b] = rd + [k]

        st_done = [None] * 4
        def rec_state(c):
            b, w = bank()
            P = banks[b]

            def go(e, c=c, P=P):
                r = slice((c % 2) * 64, (c % 2) * 64 + 64)
                for h in range(4):
                    i = mm(e, P[:, h * 128:h * 128 + 128], ks8[r, 2 * h + c // 2, :],
                           HI3[r, c // 2, h * 128:h * 128 + 128], True, True)
                return i
            t = pe(go, w, ks_done, keep["hi"])
            if c == 0:
                s = act(lambda e, P=P: e.copy(prev[:, 0:512], P[:, :]), t)
            else:
                for h in range(4):
                    s_ = dve(lambda e, c=c, h=h, P=P: e.scalar_tensor_tensor(
                        prv[:, c, h, :], prv[:, c - 1, h, :], dec[:, 4 * h + c:4 * h + c + 1],
                        P[:, h * 128:h * 128 + 128], ALU.mult, ALU.add), t, st_done[c], e3)
                s = s_
            st_done[c + 1] = s
            bank_read[b] = [s]

        rss = small(8)
        rec_done = []

        def rec_out():
            rec_banks = []
            for tt in range(2):
                b, w = bank()
                P = banks[b]

                def go(e, tt=tt, P=P):
                    for h in range(4):
                        hv = slice(h * 128, h * 128 + 128)
                        i = mm(e, P[:, hv], att8[:, 2 * h + tt, :], HI3[:, tt, hv], True, False, skip_group_check=True)
                        for c in (2 * tt, 2 * tt + 1):
                            if c:
                                i = mm(e, P[(c % 2) * 64:(c % 2) * 64 + 64, hv], E1h[:, h, c * 64:c * 64 + 64],
                                       prv[:, c - 1, h, :], False, c % 2 == 1, skip_group_check=True)
                    return i
                t = pe(go, w, att_done, st_done[2 * tt + 1], keep["hi"])
                for h in range(4):
                    hv = slice(h * 128, h * 128 + 128)
                    sq = act(lambda e, tt=tt, h=h, P=P, hv=hv: e.activation(
                        XN3[:, tt, hv], P[:, hv], ACT.Square, accum_out=rss[:, 4 * tt + h:4 * tt + h + 1]), t)
                rec_banks.append((b, P, sq))
            s = dve(lambda e: e.tensor_scalar(rss, rss, 1.0 / 128, 1e-6, ALU.mult, ALU.add), [r[2] for r in rec_banks])
            s = act(lambda e: e.activation(rss, rss, ACT.Sqrt), s)
            s_r = dve(lambda e: e.reciprocal(rss, rss), s)
            for tt in range(2):
                b, P, _ = rec_banks[tt]
                for h in range(4):
                    hv = slice(h * 128, h * 128 + 128)
                    s = dve(lambda e, tt=tt, h=h, P=P, hv=hv: e.scalar_tensor_tensor(
                        XN3[:, tt, hv], P[:, hv], rss[:, 4 * tt + h:4 * tt + h + 1], SHG3[:, tt, hv], ALU.mult,
                        ALU.mult), s_r, keep["hg"])
                bank_read[b] = [s]
                rec_done.append(s)

        mix_ready = []

        def rec_transposes():
            for hp in range(2):
                b, w = bank()
                P = banks[b]

                def go(e, hp=hp, P=P):
                    for k in range(2):
                        for t in range(2):
                            h = 2 * hp + k
                            i = e.transpose(P[:, k * 256 + t * 128:k * 256 + t * 128 + 128],
                                            XN3[:, t, h * 128:h * 128 + 128], ident)
                    return i
                t = pe(go, w, rec_done)
                r = split2([x[:, (4 + 2 * hp) * 256:(6 + 2 * hp) * 256] for x in (XTh, XTl)], P[:, :], t, p_last,
                           par("hgn"))
                bank_read[b] = [r]
                mix_ready.append(r)

        qT = [x.rearrange("p (g t) -> p g t", g=4) for x in qkT]
        qkt_ready = []
        for i in range(2):
            q3 = qk[i].rearrange("p (t d) -> p t d", t=2)
            for gp in range(2):
                b, w = bank()
                P = banks[b]

                def go(e, q3=q3, gp=gp, P=P):
                    for k in range(2):
                        for t in range(2):
                            g = 2 * gp + k
                            i = e.transpose(P[:, k * 256 + t * 128:k * 256 + t * 128 + 128],
                                            q3[:, t, g * 128:g * 128 + 128], ident)
                    return i
                t = pe(go, w, att_ready[i])
                r = act(lambda e, i=i, gp=gp, P=P: e.copy(qkT[i][:, gp * 512:gp * 512 + 512], P[:, :]), t)
                bank_read[b] = [r]
                qkt_ready.append(r)
        V3 = V.rearrange("p (t d) -> p t d", t=2)
        abias = con("abias")
        nmax, aden = small(16), small(16)
        pb_free, pt_free = [None] * NP, [None] * NP
        heads = []

        def scores(h):
            r = slice((h % 2) * 64, (h % 2) * 64 + 64)
            hp = h // 2
            b, w = bank()
            P = banks[b]

            def go(e):
                mm(e, P[:, 0:128], qT[0][r, hp, 0:128], qT[1][r, hp, 0:128], True, True)
                return mm(e, P[:, 128:384], qT[0][r, hp, 128:256], qT[1][r, hp, :], True, True)
            t = pe(go, w, qkt_ready)
            p = PB[h % NP]
            s = dve(lambda e: e.scalar_tensor_tensor(p, P[:, 0:384], 0.125, abias, ALU.mult, ALU.add), t,
                    pb_free[h % NP])
            bank_read[b] = [s]
            m0 = dve(lambda e: e.tensor_reduce(nmax[:, 2 * h:2 * h + 1], p[:, 0:128], AX, ALU.max, negate=True), s)
            m1 = dve(lambda e: e.tensor_reduce(nmax[:, 2 * h + 1:2 * h + 2], p[:, 128:384], AX, ALU.max,
                                               negate=True), s)
            x0 = act(lambda e: e.activation(p[:, 0:128], p[:, 0:128], ACT.Exp, bias=nmax[:, 2 * h:2 * h + 1],
                                            accum_out=aden[:, 2 * h:2 * h + 1]), m0)
            x1 = act(lambda e: e.activation(p[:, 128:384], p[:, 128:384], ACT.Exp, bias=nmax[:, 2 * h + 1:2 * h + 2],
                                            accum_out=aden[:, 2 * h + 1:2 * h + 2]), m1)
            s = dve(lambda e: e.reciprocal(aden[:, 2 * h:2 * h + 2], aden[:, 2 * h:2 * h + 2]), x0, x1)
            n0 = dve(lambda e: e.tensor_scalar(p[:, 0:128], p[:, 0:128], aden[:, 2 * h:2 * h + 1], None, ALU.mult), s)
            n1 = dve(lambda e: e.tensor_scalar(p[:, 128:384], p[:, 128:384], aden[:, 2 * h + 1:2 * h + 2], None,
                                               ALU.mult), s)
            return n1

        def turn_p(h, ready):
            p = PB[h % NP]
            b, w = bank()
            P = banks[b]

            def go(e):
                for j in range(3):
                    i = e.transpose(P[:, j * 128:j * 128 + 128], p[:, j * 128:j * 128 + 128], ident)
                return i
            t = pe(go, w, ready)
            pb_free[h % NP] = t
            r = act(lambda e: e.copy(PT[h % NP], P[:, 0:384]), t, pt_free[h % NP])
            bank_read[b] = [r]
            return r

        pv_bank = [None]

        def pv(h, ready):
            if h % 2 == 0:
                pv_bank[0] = bank()
            b, w = pv_bank[0]
            P = banks[b]
            o_ = slice((h % 2) * 64, (h % 2) * 64 + 64)
            hv = slice(h * 64, h * 64 + 64)
            p = PT[h % NP]

            def go(e):
                mm(e, P[o_, 0:128], V3[:, 0, hv], p[:, 0:128], True, True)
                mm(e, P[o_, 128:256], V3[:, 0, hv], p[:, 128:256], True, False)
                return mm(e, P[o_, 128:256], V3[:, 1, hv], p[:, 256:384], False, True)
            t = pe(go, w if h % 2 == 0 else None, ready, keep["v"])
            pt_free[h % NP] = t
            if h % 2:
                r = split2(both(XT3, lambda x: x[:, h // 2, :]), P[:, 0:256], t, p_last)
                bank_read[b] = [r]
                mix_ready.append(r)

        between = {0: [lambda: rec_head(0), lambda: rec_head(1)], 1: [lambda: rec_head(2), lambda: rec_head(3)],
                   2: [lambda: rec_state(0)], 3: [lambda: rec_state(1)], 4: [lambda: rec_state(2)], 5: [rec_out],
                   8: [rec_transposes]}
        sc_r, tp_r = {}, {}
        for i in range(8 + 2):
            if i < 8:
                sc_r[i] = scores(i)
            if 1 <= i <= 8:
                tp_r[i - 1] = turn_p(i - 1, sc_r[i - 1])
            if i >= 2:
                pv(i - 2, tp_r[i - 2])
            for step in between.get(i, []):
                step()
        d = down_proj(a["w_out"], XT3, mix_ready)
        x_ready = add_acc(None, 1.0, d)

        tables_ready = tables(x_ready)
        xt = rms_transpose(x_ready, par("n2"), None, None)
        d = ffn(a["ffn2_w13"], a["ffn2_w2"], 11, xt)
        x_ready = add_acc(None, 0.5, d)

        GB = XN
        bst = small(24)
        mv = small(4)
        rstd = small(2)

        def layer_norm(i, x_ready, xn_free):
            l_g = load(GB[:, 0:1024], a["ln_g"][i].partition_broadcast(128), xn_free)
            l_b = load(GB[:, 1024:2048], a["ln_b"][i].partition_broadcast(128), xn_free)
            st = bst.rearrange("p (t h s) -> p t h s", t=2, h=2)
            mv2 = mv.rearrange("p (t s) -> p t s", t=2)
            for t in range(2):
                for h in range(2):
                    s = dve(lambda e, t=t, h=h: e.bn_stats(st[:, t, h, :], X3[:, t, h * 512:h * 512 + 512]),
                            x_ready)
            for t in range(2):
                s_ = dve(lambda e, t=t: e.bn_aggr(mv2[:, t, :], st[:, t, :, :]), s)
            s = dve(lambda e: e.tensor_scalar(rstd, mv2[:, :, 1], 1e-5, None, ALU.add), s_)
            s = act(lambda e: e.activation(rstd, rstd, ACT.Sqrt), s)
            s = dve(lambda e: e.reciprocal(rstd, rstd), s)
            out = []
            for t, eng in ((0, pool), (1, dve)):
                n_ = dve(lambda e, t=t: e.tensor_scalar(X3[:, t, :], X3[:, t, :], mv2[:, t, 0:1], rstd[:, t:t + 1],
                                                        ALU.subtract, ALU.mult), s)
                m_ = dve(lambda e, t=t: e.tensor_tensor(X3[:, t, :], X3[:, t, :], GB[:, 0:1024], ALU.mult), n_, l_g)
                out.append(eng(lambda e, t=t: e.tensor_tensor(X3[:, t, :], X3[:, t, :], GB[:, 1024:2048], ALU.add),
                               m_, l_b))
            return out

        def state_space(xt):
            carve = phase(FB)
            uT, vT = XN[:, 0:1024], XN[:, 1024:2048]
            yh, yl = carve(1024, F32R), carve(1024, F32R)
            ygs = [x.rearrange("p (k t) -> p k t", k=4) for x in (yh, yl)]
            NB = 3
            at0 = carve.at[0]
            BU, PA, PBB, WW = ([carve(512), carve(512)] for _ in range(4))
            for n, x in enumerate((BU, PA, PBB, WW)):
                x.append(place(f"scan{n}", xt_at + 512 * n + (1024 if n > 1 else 0), 512))
            pa, pb_ = (place(f"pool_sum{i}", rest + at0 - 2048 + 1024 * i, 1024) for i in range(2))
            sg = place("glu", rest + at0, 1024)
            ZZ, P1, P2 = PA, PBB, BU
            yg = vT
            uT3 = uT.rearrange("p (k t) -> p k t", k=4)
            vT3 = vT.rearrange("p (k t) -> p k t", k=4)
            yg3 = yg.rearrange("p (k t) -> p k t", k=4)
            got = {}

            def project(half):
                def evac(g, P, d):
                    dst = (uT, vT)[half][:, g * 512:g * 512 + 512]
                    got[2 * half + g] = act(lambda e: e.copy(dst, P[:, :]), d)
                    return [got[2 * half + g]]
                return proj_T(a["ab_in"][2 * half:2 * half + 2], XT3, xt if half == 0 else None, evac)
            low, pool_done = [], []

            def windows():
                pb4 = [x.rearrange("p (k t) -> p k t", k=4) for x in (pa, pb_)]
                src, ready = vT3, [got[2], got[3]]
                level = []
                for l in range(4):
                    s, dst = 1 << l, pb4[l % 2]
                    c1 = dve(lambda e, l=l, s=s, dst=dst, src=src: e.tensor_copy(dst[:, l:, 0:s], src[:, l:, 0:s]), ready)
                    c2 = dve(lambda e, l=l, s=s, dst=dst, src=src: e.tensor_tensor(
                        dst[:, l:, s:], src[:, l:, s:], src[:, l:, 0:T - s], ALU.add))
                    m1 = dve(lambda e, l=l, dst=dst: e.tensor_tensor(
                        dst[:, l, 0:16], dst[:, l, 0:16], con("invc", 16 * l, 16), ALU.mult), c2)
                    m2 = dve(lambda e, l=l, dst=dst: e.tensor_scalar(
                        dst[:, l, 16:], dst[:, l, 16:], 0.5 ** (l + 1), None, ALU.mult))
                    m3 = dve(lambda e, l=l, dst=dst: e.tensor_tensor(yg3[:, l, :], dst[:, l, :], vT3[:, l, :],
                                                                      ALU.subtract), m2)
                    level.append(m3)
                    src, ready = dst, [m3]
                low.append(split2((yh, yl), vT, level))

            def mix_windows():
                blk = Block(a["pool_w"])
                pw = blk.view(k=4)
                for gp in range(2):
                    b, w = bank()
                    P = banks[b]

                    def go(e, gp=gp, P=P):
                        for k in range(2):
                            g = 2 * gp + k
                            i = mm3(e, P[:, k * 256:k * 256 + 256], both(pw, lambda x: x[:, g, :]),
                                    both(ygs, lambda x: x[:, g, :]), True, True)
                        return i
                    t = pe(go, w, blk.here, low)
                    for k in range(2):
                        g = 2 * gp + k
                        r = split2(both(XT3, lambda x: x[:, 4 + g, :]), P[:, k * 256:k * 256 + 256], [t, r] if k else t,
                                   p_last, par("ps", g, 1))
                    bank_read[b] = [r]
                    pool_done.append(r)
                blk.done(t)
                pump()

            bre = par("bre").rearrange("p (q n) -> p q n", q=4)
            bim = par("bim").rearrange("p (q n) -> p q n", q=4)
            free = [dict() for _ in range(NB)]
            y_bank = [None]
            yg_done = []
            stage = []

            def first(j, p_last=None):
                q, r = j // 4, slice(32 * (j % 4), 32 * (j % 4) + 32)
                f = free[j % NB]
                b, w = bank()
                P = banks[b]

                def go(e):
                    mm(e, P[:, 0:256], bre[r, q, :], uT3[r, q, :], True, True)
                    return mm(e, P[:, 256:512], bim[r, q, :], uT3[r, q, :], True, True)
                t = pe(go, w, got[0], got[1])
                bu, pA, pB, ww, zz, p1, p2 = (x[j % NB] for x in (BU, PA, PBB, WW, ZZ, P1, P2))
                csj = CS[:, 512 * j:512 * j + 512]
                cj, sj = csj[:, 0:256], csj[:, 256:512]
                cp = act(lambda e: e.copy(bu, P[:, :]), t, f.get("pe"), p_last)
                m1 = dve(lambda e: e.tensor_tensor(pA, P[:, :], csj, ALU.mult), cp, f.get("zz"), tables_ready, p_last)
                bank_read[b] = [cp, m1]
                m2 = pool(lambda e: e.tensor_tensor(pB[:, 0:256], bu[:, 256:512], cj, ALU.mult), cp, f.get("pe"), p_last)
                m3 = pool(lambda e: e.tensor_tensor(pB[:, 256:512], bu[:, 0:256], sj, ALU.mult))
                w1 = dve(lambda e: e.tensor_tensor(ww[:, 0:256], pA[:, 0:256], pA[:, 256:512], ALU.add), m1,
                         f.get("ww"))
                rj = mag[:, j:j + 1].to_broadcast([128, 256])
                z1 = dve(lambda e: e.tensor_tensor_scan(zz[:, 0:256], rj, ww[:, 0:256], 0.0, ALU.mult, ALU.add), w1)
                w2 = dve(lambda e: e.tensor_tensor(ww[:, 256:512], pB[:, 0:256], pB[:, 256:512], ALU.subtract),
                         m3, f.get("ww"))
                z2 = dve(lambda e: e.tensor_tensor_scan(zz[:, 256:512], rj, ww[:, 256:512], 0.0, ALU.mult, ALU.add),
                         w2)
                f["ww"] = z2
                a1 = dve(lambda e: e.tensor_tensor(p1, zz, csj, ALU.mult), z2, w2)
                a2 = pool(lambda e: e.tensor_tensor(p2[:, 0:256], zz[:, 0:256], sj, ALU.mult), z2)
                a3 = pool(lambda e: e.tensor_tensor(p2[:, 256:512], zz[:, 256:512], cj, ALU.mult))
                f["zz"] = [a1, a3]
                return [a1, a3]

            def second(j, ready):
                q = j // 4
                if j % 4 == 0:
                    y_bank[0] = bank()
                    held.add(y_bank[0][0])
                b, w = y_bank[0]
                P = banks[b]
                o_ = slice(32 * (j % 4), 32 * (j % 4) + 32)
                p1, p2 = P1[j % NB], P2[j % NB]

                def go(e):
                    mm(e, P[o_, 0:256], CM3[0][:, j, :], p1[:, 0:256], True, False)
                    mm(e, P[o_, 0:256], CM3[1][:, j, :], p1[:, 256:512], False, False)
                    mm(e, P[o_, 0:256], CM3[2][:, j, :], p2[:, 0:256], False, False)
                    return mm(e, P[o_, 0:256], CM3[2][:, j, :], p2[:, 256:512], False, True)
                t = pe(go, w if j % 4 == 0 else None, ready)
                free[j % NB]["pe"] = t
                if j % 4 == 3:
                    held.discard(b)
                    s = dve(lambda e: e.scalar_tensor_tensor(yg3[:, q, :], uT3[:, q, :], par("sd", q, 1), P[:, 0:256],
                                                             ALU.mult, ALU.add), t, pool_done)
                    bank_read[b] = [s]
                    s = act(lambda e: e.activation(yg3[:, q, :], yg3[:, q, :], ACT.Gelu_apprx_tanh), s)
                    yg_done.append(split2(both(ygs, lambda x: x[:, q, :]), yg3[:, q, :], s))
            project(0)
            stage.extend([first(0), first(1)])
            p_last = project(1)
            stage.append(first(2, p_last))
            windows()
            for j in range(3, 19):
                if j == 5:
                    mix_windows()
                second(j - 3, stage[j - 3])
                if j < 16:
                    stage.append(first(j))
            blk = Block(a["w_glu"])
            wg = blk.view(k=4)
            cat_done = list(pool_done)
            for mp in range(2):
                b, w = bank()
                P = banks[b]

                def go(e, mp=mp, P=P):
                    for c in range(2):
                        m = 2 * mp + c
                        for k in range(4):
                            i = mm3(e, P[:, c * 256:c * 256 + 256], both(wg, lambda x: x[:, k, m * 128:m * 128 + 128]),
                                    both(ygs, lambda x: x[:, k, :]), k == 0, k == 3)
                    return i
                t = pe(go, w, blk.here, yg_done)
                dst = sg[:, mp * 512:mp * 512 + 512]
                s = act(lambda e, dst=dst, P=P: e.activation(dst, P[:, :], ACT.Sigmoid), t, [x["pe"] for x in free])
                bank_read[b] = [s]
                s = dve(lambda e, dst=dst, mp=mp: e.tensor_tensor(
                    dst, dst, yg[:, mp * 512:mp * 512 + 512], ALU.mult), s)
                cat_done.append(split2([x[:, mp * 512:mp * 512 + 512] for x in (XTh, XTl)], dst, s))
            blk.done(t)
            pump()
            return down_proj(a["ab_out"], XT3, cat_done), cat_done

        def stick_breaking(xt):
            carve = phase()
            V = carve(2048)
            qT, kT = [carve(512) for _ in range(2)], [carve(512) for _ in range(2)]
            OT = carve(2048, F32R), carve(2048, F32R)
            ZS = [carve(384) for _ in range(12)]
            LL = [carve(384) for _ in range(8)]
            OT3 = both(OT, lambda x: x.rearrange("p (k t) -> p k t", k=8))
            V3 = V.rearrange("p (t d) -> p t d", t=2)
            v_ready, qk_ready = [], {}
            for h in range(2):
                def evac_v(t, P, d, h=h):
                    r = act(lambda e: e.copy(V3[:, t, h * 512:h * 512 + 512], P[:, :]), d)
                    v_ready.append(r)
                    return [r]
                proj_tok(a["sb_v"][h], xt, evac_v)
            tri, ones = con("tri"), con("ones")
            strict2 = con("strict").unsqueeze(1).to_broadcast([128, 2, 128])
            neg2 = con("neg").unsqueeze(1).to_broadcast([128, 2, 128])

            def diag(x):
                return x[:, 0:384].rearrange("p (c t) -> p c t", c=3)[:, 0:3:2, :]

            def project(g):
                def evac_q(_, P, d):
                    qk_ready[g] = [act(lambda e: e.activation(qT[g % 2], P[:, :], ACT.Copy, scale=0.125), d)]
                    return qk_ready[g][:]

                def evac_k(_, P, d):
                    qk_ready[g].append(dve(lambda e: e.tensor_copy(kT[g % 2], P[:, :]), d))
                    return qk_ready[g][1:]
                proj_T(a["sb_q"][g:g + 1], XT3, None, evac_q)
                proj_T(a["sb_k"][g:g + 1], XT3, None, evac_k)

            z_free, l_free, l_ready, w_ready, o_ready = {}, {}, {}, {}, {}

            def scores(g):
                q3, k3 = (x[g % 2].rearrange("p (k t) -> p k t", k=2) for x in (qT, kT))
                heads = range(4 * g, 4 * g + 4)
                zs, es = {}, {}
                for h in heads:
                    r, hp = slice((h % 2) * 64, (h % 2) * 64 + 64), h % 4 // 2
                    b, w = bank()
                    P = banks[b]

                    def go(e, r=r, hp=hp, P=P):
                        mm(e, P[:, 0:256], k3[r, hp, 0:128], q3[r, hp, :], True, True)
                        return mm(e, P[:, 256:384], k3[r, hp, 128:256], q3[r, hp, 128:256], True, True)
                    t = pe(go, w, qk_ready[g])
                    zs[h] = dve(lambda e, h=h, P=P: e.tensor_copy(ZS[h % 12], P[:, 0:384]), t, z_free.get(h - 12))
                    bank_read[b] = [zs[h]]
                for h in heads:
                    es[h] = act(lambda e, h=h: e.activation(LL[h % 8], ZS[h % 12], ACT.Abs), zs[h], l_free.get(h - 8))
                for h in heads:
                    es[h] = act(lambda e, h=h: e.activation(LL[h % 8], LL[h % 8], ACT.Exp, scale=-1.0), es[h])
                return es

            def logs(g, es):
                for h in range(4 * g, 4 * g + 4):
                    x = act(lambda e, h=h: e.activation(LL[h % 8], LL[h % 8], ACT.Ln, bias=1.0), es[h])
                    x = dve(lambda e, h=h: e.scalar_tensor_tensor(LL[h % 8], ZS[h % 12], 0.0, LL[h % 8], ALU.max,
                                                                  ALU.add), x)
                    l_ready[h] = pool(lambda e, h=h: e.tensor_tensor(diag(LL[h % 8]), diag(LL[h % 8]), strict2,
                                                                     ALU.mult), x)

            def sums(g, first=0):
                for h in range(4 * g, 4 * g + 4):
                    b, w = bank(first)
                    P = banks[b]
                    z, ll = ZS[h % 12], LL[h % 8]

                    def go(e, P=P, ll=ll):
                        mm(e, P[:, 256:384], tri, ll[:, 256:384], True, True)
                        mm(e, P[:, 0:256], tri, ll[:, 0:256], True, False, skip_group_check=True)
                        return mm(e, P[:, 128:256], ones, ll[:, 256:384], False, True, skip_group_check=True)
                    l_free[h] = t = pe(go, w, l_ready[h])
                    s = dve(lambda e, z=z, P=P: e.tensor_tensor(z, z, P[:, 0:384], ALU.subtract), t)
                    bank_read[b] = [s]
                    w_ready[h] = pool(lambda e, z=z: e.tensor_tensor(diag(z), diag(z), neg2, ALU.add), s)

            def weights(g):
                for h in range(4 * g, 4 * g + 4):
                    w_ready[h] = act(lambda e, h=h: e.activation(ZS[h % 12], ZS[h % 12], ACT.Exp), w_ready[h])

            def values(g, first=0):
                o_ready[g] = []
                for hp in range(2 * g, 2 * g + 2):
                    b, w = bank(first)
                    P = banks[b]

                    def go(e, hp=hp, P=P):
                        for h in (2 * hp, 2 * hp + 1):
                            o_, hv, ww = slice((h % 2) * 64, (h % 2) * 64 + 64), slice(h * 64, h * 64 + 64), ZS[h % 12]
                            mm(e, P[o_, 0:256], V3[:, 0, hv], ww[:, 0:256], True, False, skip_group_check=True)
                            i = mm(e, P[o_, 128:256], V3[:, 1, hv], ww[:, 256:384], False, True, skip_group_check=True)
                        return i
                    t = pe(go, w, w_ready[2 * hp], w_ready[2 * hp + 1], v_ready)
                    z_free[2 * hp] = z_free[2 * hp + 1] = t
                    r = split2(both(OT3, lambda x: x[:, hp, :]), P[:, 0:256], t)
                    bank_read[b] = [r]
                    o_ready[g].append(r)

            for g in range(4):
                project(g)
                if g >= 2:
                    values(g - 2)
                if g >= 1:
                    sums(g - 1)
                es = scores(g)
                if g >= 1:
                    weights(g - 1)
                logs(g, es)
            sums(3, 4)
            values(2, 4)
            weights(3)
            return down_proj(a["sb_out"], OT3, o_ready, between={2: lambda: values(3, 4)})

        sco, sel, rank, mask, gat = (small(32) for _ in range(5))
        gsc, grk = small(8), small(8)
        slot_gate, own_gate = small(16), small(16)
        gah, gal = gsplit[:, 0:32], gsplit[:, 32:64]
        wsum = small(2)
        low = con("lower").rearrange("p (i j) -> p i j", i=4)

        def router(xt):
            carve = phase(6144)
            cmp1, cmp2 = carve(128), carve(128)
            b, w = bank()
            P = banks[b]
            rw2 = both((rwh, rwl), lambda x: x.rearrange("p (k e) -> p k e", k=8))

            def go(e):
                for t in range(2):
                    for k in range(8):
                        i = mm3(e, P[:, t * 16:t * 16 + 16], both(XT3, lambda x: x[:, k, t * 128:t * 128 + 128]),
                                both(rw2, lambda x: x[:, k, :]), k == 0, k == 7)
                return i
            t = pe(go, w, xt, rw_ready)
            s = act(lambda e: e.activation(sco, P[:, 0:32], ACT.Sigmoid), t)
            bank_read[b] = [s]
            v4 = sel.rearrange("p (g i) -> p g i", i=4)
            sc3 = sco.rearrange("p (t e) -> p t e", t=2)
            sel3 = sel.rearrange("p (t e) -> p t e", t=2)
            s = dve(lambda e: e.tensor_tensor(sel3, sc3, par("rb").unsqueeze(1).to_broadcast([128, 2, 16]), ALU.add), s)
            m3 = mask.rearrange("p (g i) -> p g i", i=4)
            c1 = cmp1.rearrange("p (g i j) -> p g i j", i=4, j=4)
            c2 = cmp2.rearrange("p (g i j) -> p g i j", i=4, j=4)

            def ranks(v, groups, out, s):
                vj = v.unsqueeze(2).to_broadcast([128, groups, 4, 4])
                vi = v.unsqueeze(3).to_broadcast([128, groups, 4, 4])
                lw = low.unsqueeze(1).to_broadcast([128, groups, 4, 4])
                x, y = c1[:, 0:groups, :, :], c2[:, 0:groups, :, :]
                s1 = dve(lambda e: e.tensor_tensor(x, vj, vi, ALU.is_gt), s)
                s2 = dve(lambda e: e.tensor_tensor(y, vj, vi, ALU.is_equal), s)
                s3 = dve(lambda e: e.tensor_tensor(y, y, lw, ALU.mult), s2)
                s4 = dve(lambda e: e.tensor_tensor(x, x, y, ALU.add), s3)
                return dve(lambda e: e.tensor_reduce(out, x, AX, ALU.add), s4)
            s = ranks(v4, 8, rank.rearrange("p (g i) -> p g i", i=4), s)
            s = dve(lambda e: e.tensor_scalar(mask, rank, 2.0, None, ALU.is_lt), s)
            s = dve(lambda e: e.tensor_tensor(rank, mask, sel, ALU.mult), s)
            s = dve(lambda e: e.tensor_reduce(gsc, rank.rearrange("p (g i) -> p g i", i=4), AX, ALU.add), s)
            s = ranks(gsc.rearrange("p (t g) -> p t g", t=2), 2, grk.rearrange("p (t g) -> p t g", t=2), s)
            s = dve(lambda e: e.tensor_scalar(grk, grk, 1.0, None, ALU.is_lt), s)
            s = dve(lambda e: e.tensor_tensor(m3, m3, grk.unsqueeze(2).to_broadcast([128, 8, 4]), ALU.mult), s)
            s = dve(lambda e: e.tensor_tensor(gat, mask, sco, ALU.mult), s)
            g3 = gat.rearrange("p (t e) -> p t e", t=2)
            s = dve(lambda e: e.tensor_reduce(wsum, g3, AX, ALU.add), s)
            s = dve(lambda e: e.reciprocal(wsum, wsum), s)
            s = dve(lambda e: e.tensor_tensor(g3, g3, wsum.unsqueeze(2).to_broadcast([128, 2, 16]), ALU.mult), s)
            o = act(lambda e: e.copy(gah, gat), s)
            return s, dve(lambda e: e.tensor_tensor(gal, gat, gah.bitcast(F32), ALU.subtract), o)

        def places(i, gates_ready):
            Pm, PD = place(f"places{i}", rest + 2048, 2048, F32R), place(f"pairs{i}", rest + 10240, 4096, F32R)
            mask2 = mask.rearrange("p (t e) -> p t e", t=2)
            b, w = bank(4)
            P = banks[b]

            def go(e):
                mm(e, P[:, 0:16], con("strict"), mask2[:, 0, :], True, True)
                mm(e, P[:, 16:32], con("ones"), mask2[:, 0, :], True, False)
                mm(e, P[:, 16:32], con("strict"), mask2[:, 1, :], False, True)
                for t in range(2):
                    j = mm(e, P[:, 32:48], con("ones"), mask2[:, t, :], t == 0, t == 1)
                return j
            t = pe(go, w, gates_ready)
            s = dve(lambda e: e.tensor_reduce(wsum[:, 0:1], P[:, 32:48], AX, ALU.max), t, gates_ready)
            flag_ready = dve(lambda e: e.tensor_copy(flag, wsum[:, 0:1]), s)
            s = dve(lambda e: e.tensor_scalar(rank, mask, -1000.0, 1000.0, ALU.mult, ALU.add), gates_ready)
            s = dve(lambda e: e.tensor_tensor(rank, rank, P[:, 0:32], ALU.add), t, s)
            bank_read[b] = [s]
            P4 = Pm.rearrange("p (t e c) -> p t e c", t=2, e=16)
            iota = con("iota").unsqueeze(1).to_broadcast([128, 16, 64])
            oh = []
            for t in range(2):
                at = rank[:, 16 * t:16 * t + 16].unsqueeze(2).to_broadcast([128, 16, 64])
                oh.append(dve(lambda e, t=t, at=at: e.tensor_tensor(P4[:, t, :, :], iota, at, ALU.is_equal), s))
            PD5 = PD.rearrange("p (t x h n) -> p t x h n", t=2, x=16, h=2)
            pd = [eng(lambda e, t=t, copy=copy: copy(e)(PD5[:, t, :, :, :], P4[:, t, :, :].bitcast(F32).unsqueeze(2)
                                                        .to_broadcast([128, 16, 2, 64])), oh[t])
                  for t, eng, copy in ((0, act, lambda e: e.copy), (1, dve, lambda e: e.tensor_copy))]
            return flag_ready, Pm, PD, oh, pd

        def dense_experts(i, xt, gates_ready, before):
            carve = phase()
            GG, gT = carve(4096), carve(256)
            HT = carve(1536, F32R), carve(1536, F32R)
            assert carve.at[0] <= FB
            b, w = bank(4)
            P = banks[b]
            g3 = gat.rearrange("p (t e) -> p t e", t=2)

            def go(e):
                for t in range(2):
                    i = e.transpose(P[0:16, t * 128:t * 128 + 128], g3[:, t, :], ident)
                return i
            t = pe(go, w, gates_ready)
            gt_done = dve(lambda e: e.tensor_copy(gT[0:16, :], P[0:16, 0:256]), t, before)
            bank_read[b] = [gt_done]
            ready = []
            for ep in range(8):
                b, w = bank(4)
                P = banks[b]

                def go(e, ep=ep, P=P):
                    for k in range(2):
                        x = 2 * ep + k
                        i = mm(e, P[:, k * 256:k * 256 + 256], ident[0:16, x:x + 1].to_broadcast([16, 128]),
                               gT[0:16, :], True, True)
                    return i
                t = pe(go, w, gt_done)
                r = act(lambda e, ep=ep, P=P: e.copy(GG[:, 512 * ep:512 * ep + 512], P[:, :]), t, before)
                bank_read[b] = [r]
                ready.append(r)
            ffn(a["moe_w13"][i], a["moe_w2"][i], 32, xt, lambda x: (GG[:, 256 * x:256 * x + 256], ready[x // 2]),
                2, HT, before)

        def sparse_experts(i, gates_ready, x_split, tables, ple_done):
            w13, w2 = a["moe_w13"][i], a["moe_w2"][i]
            carve = phase()
            _, Pm, PD, oh, pd = tables
            carve(4096)
            SG = carve(4096, F32R)
            XG = [carve(2048, F32R) for _ in range(2)]
            Y = carve(1024, F32R), carve(1024, F32R)
            S = [carve(512) for _ in range(2)]
            hs = [carve(128) for _ in range(2)]
            HP = [carve(256, F32R) for _ in range(2)]
            Pm3 = Pm.rearrange("p (t n) -> p t n", t=2)
            SG3 = SG.rearrange("p (x t) -> p x t", x=16)
            X2 = both(x_split[0], lambda x: x.rearrange("p (t d) -> p t d", t=2))
            XG5 = [x.rearrange("p (r k h n) -> p k r h n", r=2, k=8, h=2) for x in XG]
            xg_ready = {}

            PD3 = PD.rearrange("p (t x n) -> p t x n", t=2, x=16)

            def gather(e, P, p, ks):
                for n, k in enumerate(ks):
                    for t in range(2):
                        for x in range(2):
                            j = mm(e, P[:, n * 128:n * 128 + 128], X2[x][:, t, k * 128:k * 128 + 128],
                                   Pm3[:, t, p * 128:p * 128 + 128], t == 0 and x == 0, t == 1 and x == 1)
                return j

            def gathered(p, ks, P, ready):
                src = P.rearrange("p (k r n) -> p k r n", r=2, n=64)
                dst = [XG5[p % 2][:, ks[0]:ks[-1] + 1, :, x, :] for x in range(2)]
                c = act(lambda e: e.copy(dst[0], src), ready)
                return c, lambda *after: xg_ready.setdefault(p, []).append(dve(lambda e: e.tensor_tensor(
                    dst[1], src, dst[0].bitcast(F32), ALU.subtract), c, *after))

            def gather_first(p, ks):
                b, w = bank(4)
                P = banks[b][:, 0:128 * len(ks)]
                t = pe(lambda e: gather(e, P, p, ks), w, oh, x_split[1])
                gathered(p, ks, P, t)[1]()
                bank_read[b] = [xg_ready[p][-1]]

            for half in range(2):
                gather_first(0, range(4 * half, 4 * half + 4))
            sg_ready = []
            for q in range(8):
                b, w = bank(4)

                def go(e, q=q, P=banks[b]):
                    for k in range(2):
                        for t in range(2):
                            j = mm(e, P[:, k * 256 + t * 128:k * 256 + t * 128 + 128], PD3[:, t, 2 * q + k, :], identr,
                                   True, True)
                    return j
                t = pe(go, w, pd, ident_split)
                dst = SG[:, q * 512:q * 512 + 512]
                if q % 2:
                    c = act(lambda e, dst=dst, P=banks[b]: e.copy(dst, P[:, :]), t, ple_done)
                else:
                    c = dve(lambda e, dst=dst, P=banks[b]: e.tensor_copy(dst, P[:, :]), t, ple_done)
                bank_read[b] = [c]
                sg_ready.append(c)
            def gates(b):
                P = banks[b]
                w, bank_read[b] = bank_read[b], []

                def go(e):
                    for p in range(8):
                        for t in range(2):
                            for x in range(2):
                                j = mm(e, P[:, p * 16:p * 16 + 16], Pm3[:, t, p * 128:p * 128 + 128],
                                       (gah, gal)[x][:, 16 * t:16 * t + 16], t == 0 and x == 0, t == 1 and x == 1)
                    return j
                t = pe(go, w, oh, gates_ready)
                z = dve(lambda e: e.memset(own_gate, 0.0))
                o = [dve(lambda e, r=r: e.tensor_copy(own_gate[64 * r:64 * r + 64, r:16:2],
                                                      P[64 * r:64 * r + 64, r:r + 127:18]), t, z) for r in range(2)]
                t = pe(lambda e: mm(e, P[:, 128:144], twin, own_gate, True, True), o, id2_ready)
                sg_ready.append(dve(lambda e: e.tensor_copy(slot_gate, P[:, 128:144]), t))
                bank_read[b] = [sg_ready[-1]]
            gather_first(1, range(2))
            y_ready = [[x for b in (4, 5) for x in bank_read[b]]]
            h_ready, spread_at = {}, [None]

            def up(g, c, w):
                blk = Block(w13[2 * g + c])
                p, r = g // 4, g // 2 % 2
                P = banks[6 + g % 2]
                W = blk.view(k=8)

                def go(e):
                    for k in range(8):
                        rows = XG[p % 2][:, (8 * r + k) * 128:(8 * r + k) * 128 + 128]
                        mm(e, P[:, c * 256:c * 256 + 256], rows, W[0][:, k, :], k == 0, False)
                        j = mm(e, P[:, c * 256:c * 256 + 256], rows, W[1][:, k, :], False, k == 7)
                    return j
                u = pe(go, w, blk.here, xg_ready[p])
                blk.done(u)
                return u

            def fold(g, copied):
                P = banks[6 + g % 2]
                p, part = (g + 1) // 4 + 1, (g + 1) % 4
                ks = range(2 * part, 2 * part + 2)
                more = p < 8

                def go(e):
                    for v in range(2):
                        for c in range(2):
                            j = mm(e, P[:, (2 * v + c) * 64:(2 * v + c) * 64 + 64],
                                   S[g % 2][:, (2 * c + v) * 128:(2 * c + v) * 128 + 128], ident2, True, True)
                    return gather(e, P[:, 256:512], p, ks) if more else j
                f = pe(go, copied, id2_ready)
                x = hs[g % 2]
                c = s = act(lambda e: e.activation(x, P[:, 0:128], ACT.Silu), f)
                if more:
                    c, low = gathered(p, ks, P[:, 256:512], f)
                m = dve(lambda e: e.tensor_tensor(x, x, P[:, 128:256], ALU.mult), s, c)
                bank_read[6 + g % 2] = [m]
                parts = HP[g % 2].rearrange("p (c h n) -> p h c n", c=2, h=2)
                h_ready[g] = split2((parts[:, 0, :, :], parts[:, 1, :, :]), x.rearrange("p (c n) -> p c n", c=2), m)
                if more:
                    low()
                    bank_read[6 + g % 2].append(xg_ready[p][-1])

            def down(g):
                blk = Block(w2[g])
                W = blk.view(c=2)

                def go(e):
                    for c in range(2):
                        for h in range(2):
                            for x in range(2):
                                j = mm(e, banks[4 + h][:, :], HP[g % 2][:, c * 128:c * 128 + 128],
                                       W[x][:, c, h * 512:h * 512 + 512], g % 2 == 0 and c == 0 and x == 0,
                                       g % 2 == 1 and c == 1 and x == 1)
                    return j
                d = pe(go, blk.here, h_ready[g], y_ready[-1] if g % 2 == 0 else None)
                blk.done(d)
                if g % 2:
                    x = g // 2
                    y_ready.append([split2([y[:, h * 512:h * 512 + 512] for y in Y], banks[4 + h][:, :], d,
                                           [sg_ready, spread_at[0]], slot_gate[:, x:x + 1]) for h in range(2)])

            def spread(x):
                def go(e):
                    for t in range(2):
                        for h in range(2):
                            for y in range(2):
                                j = mm(e, banks[2 * t + h][:, :], SG3[:, x, t * 128:t * 128 + 128],
                                       Y[y][:, h * 512:h * 512 + 512], x == 0 and y == 0, x == 15 and y == 1)
                    return j
                spread_at[0] = pe(go, y_ready[x + 1], bank_read[0:4] if x == 0 else None)

            copied = {}
            for g in range(34):
                if g < 32:
                    b = 6 + g % 2
                    w, bank_read[b] = bank_read[b], []
                    up(g, 0, w)
                if 1 <= g <= 32:
                    fold(g - 1, copied[g - 1])
                if g == 2:
                    gates(0)
                if g < 32:
                    u = up(g, 1, None)
                    copied[g] = act(lambda e, g=g: e.copy(S[g % 2], banks[6 + g % 2][:, :]), u)
                if g >= 2:
                    down(g - 2)
                if g % 2 == 0 and g >= 4:
                    spread(g // 2 - 2)
            spread(15)
            pump(SPLIT)

        def ple_term(i, ple, xt, between):
            d1 = down_proj(a["ple_gate"][i], XT3, xt, 0, between={0: between})
            bp = Block(a["p"][i])
            p3 = bp.view(k=2)
            d2 = down_proj(a["ple_proj"][i], p3, [bp.here], 4, 2)
            out = []
            for b in range(4):
                dst = ple[:, b * 512:b * 512 + 512]
                s = act(lambda e, b=b, dst=dst: e.activation(dst, banks[b][:, :], ACT.Sigmoid), d1)
                bank_read[b] = [s]
                m = dve(lambda e, b=b, dst=dst: e.tensor_tensor(dst, dst, banks[4 + b][:, :], ALU.mult), s, d2)
                bank_read[4 + b] = [m]
                x = X3[:, b // 2, (b % 2) * 512:(b % 2) * 512 + 512]
                out.append(dve(lambda e, x=x, dst=dst: e.scalar_tensor_tensor(x, x, ALPHA, dst, ALU.mult, ALU.add), m))
            bp.done(m)
            return out

        def experts(i, xt, gates_ready, x_split, tables, ple_done):
            arms = Q.split(flag[0:1, 0:1], CAP + 1, tables[0])
            kept = dict(state), dict(used), dict(split_done), [list(x) for x in bank_read], list(turn)
            Q.enter(arms, 0)
            sparse_experts(i, gates_ready, x_split, tables, ple_done)
            last = state["use"] - 1
            after = dict(state)
            Q.enter(arms, 1)
            state.update(kept[0])
            for x in (used, split_done):
                x.clear()
            used.update(kept[1])
            split_done.update(kept[2])
            bank_read[:] = kept[3]
            turn[:] = kept[4]
            before = [x_split[1], ple_done, tables[3:]]
            hs_read[:], hf_read[:] = [before] * 4, [before] * 4
            dense_experts(i, xt, gates_ready, before)
            pump(SPLIT)
            assert state == after, (state, after)
            ends = list(Q.leave(arms).values()) + [used[last]]
            bank_read[:] = [ends] * 8
            hs_read[:], hf_read[:] = [None] * 4, [None] * 4
            return ends

        for i in range(2):
            xt = transposes(X3, x_ready, None, None)
            if i == 0:
                d, xn_free = state_space(xt)
            else:
                d, xn_free = stick_breaking(xt), x_ready
            x_ready = add_acc(ALPHA, None, d, xt)
            x_ready = layer_norm(2 * i, x_ready, xn_free)
            XL = place(f"x_low{i}", rest, 2048, F32R)
            xt = transposes(X3, x_ready, None, None)
            mask_ready, gates_ready = router(xt)
            ple = place(f"ple{i}", rest + 4096, 2048)
            tables = []
            x_split = (XNr, XL), split2((XNr, XL), Xs, x_ready)
            ple_done = ple_term(i, ple, xt, lambda: tables.extend(places(i, mask_ready)))
            ahead[0] = AHEAD
            ends = experts(i, xt, gates_ready, x_split, tables, ple_done)
            ahead[0] = SPLIT
            x_ready = add_acc(None, 1.0, ends)
            x_ready = layer_norm(2 * i + 1, x_ready, ends)
        s_out = sem("d_out")
        Q.fixed(Q.put("sp", lambda e: e.dma_start(a["out"], X3), x_ready), s_out, 16, 16)

        Q.number(sems)
        block = ctx.enter_context(nc.Block())

        @block.sync
        def _(e):
            Q.emit("sp", e)
            e.wait_ge(s_out, 16)

        @block.tensor
        def _(e):
            Q.emit("pe", e)

        @block.scalar
        def _(e):
            Q.emit("act", e)

        @block.vector
        def _(e):
            Q.emit("dve", e)

        @block.gpsimd
        def _(e):
            Q.emit("pool", e)


def _constants():
    f = np.float32
    c = {}
    i, j = np.arange(128)[:, None], np.arange(128)[None, :]
    c["ident"] = np.eye(128, dtype=f)
    c["ones"] = np.ones((128, 128), f)
    c["tri"] = (i >= j).astype(f)
    c["strict"] = (i < j).astype(f)
    c["neg"] = np.where(i < j, 0.0, -1e30).astype(f)

    def bias(dist):
        n = ((dist >= 0) & (dist <= 128)).astype(int) + ((dist >= 0) & (dist % 4 == 0)) + ((dist >= 0) & (dist % 16 == 0))
        return np.where(n > 0, np.log(np.maximum(n, 1)), -1e30).astype(f)
    c["abias"] = np.concatenate([bias(i - j), bias(128 + i - j), bias(i - j)], axis=1)
    c["hgm"] = ((i <= j) & (i // 64 == j // 64)).astype(f)
    c["seg"] = np.broadcast_to((np.arange(256) % 64 != 0).astype(f), (128, 256))
    inv = f(500000.0) ** (-np.arange(0, 16, 2, dtype=f) / f(16))
    ang = (np.arange(256, dtype=f)[:, None] * inv[None, :]).astype(f)
    c["cos"] = np.cos(ang).astype(f).reshape(2, 128, 8).transpose(1, 0, 2).reshape(128, 16)
    c["sin"] = np.sin(ang).astype(f).reshape(2, 128, 8).transpose(1, 0, 2).reshape(128, 16)
    w = np.array([2, 4, 8, 16])[:, None]
    c["invc"] = np.broadcast_to((1.0 / np.minimum(np.arange(16)[None, :] + 1, w)).astype(f).reshape(1, 64), (128, 64))
    k = np.arange(4)
    c["lower"] = np.broadcast_to((k[None, :] < k[:, None]).astype(f).reshape(1, 16), (128, 16))
    c["iota"] = np.broadcast_to(np.arange(64, dtype=f), (128, 64))
    return np.concatenate([np.asarray(c[n], f).reshape(128, w_) for n, w_ in CONSTS], axis=1)


def _layout(inp):
    x = {k: np.asarray(v) for k, v in inp.items()}

    def colpart(v, k):
        return v.reshape(k, 128).T

    def cols(w, n):
        K, N = w.shape
        return w.reshape(K // 128, 128, N // n, n).transpose(2, 1, 0, 3).reshape(N // n, 128, K // 128 * n)

    def rows(w, k):
        K, N = w.shape
        return w.reshape(K // 128 // k, k, 128, N).transpose(0, 2, 1, 3).reshape(K // 128 // k, 128, k * N)

    def ffn(w1, w3):
        n = w1.shape[1] // 128
        return np.stack([cols(w, 128).reshape(n, 128, 8, 128) for w in (w1, w3)], axis=3).reshape(n, 128, 2048)

    o = {}
    p = {"n1": colpart(x["ffn1_norm"], 8), "nm": colpart(x["mix_norm"], 8), "n2": colpart(x["ffn2_norm"], 8),
         "lb": x["hg_lb_logits"].reshape(2, 4, 128).transpose(2, 0, 1).reshape(128, 8),
         "hgn": x["hg_out_norm"].reshape(128, 1),
         "qn": np.broadcast_to(x["q_norm"].reshape(1, 64), (128, 64)),
         "kn": np.broadcast_to(x["k_norm"].reshape(1, 64), (128, 64)),
         "lre": x["s5_lambda_re_2"].reshape(16, 128).T, "lim": x["s5_lambda_im_2"].reshape(16, 128).T,
         "ldt": np.repeat(x["s5_log_dt_2"].reshape(16, 2), 64, axis=1).T,
         "sd": x["s5_d_2"].reshape(4, 128).T, "ps": x["pool_scale_2"].reshape(4, 128).T,
         "rb": np.broadcast_to(x["router_bias_2"].reshape(1, 16), (128, 16)),
         "rw": x["router_w_2"].reshape(8, 128, 16).transpose(1, 0, 2).reshape(128, 128)}
    for n, key in (("bre", "s5_b_re_2"), ("bim", "s5_b_im_2")):
        b = x[key].reshape(4, 4, 2, 64, 16)
        z = np.zeros((4, 2, 16, 4, 2, 64), b.dtype)
        for g in range(2):
            z[:, g, :, :, g, :] = b[:, :, g].transpose(1, 3, 0, 2)
        p[n] = z.reshape(128, 512)
    o["params"] = np.concatenate([p[n].reshape(128, w) for n, w in PARAMS], axis=1)
    cc = []
    for key in ("s5_c_re_2", "s5_c_im_2"):
        c = x[key].reshape(16, 2, 16, 64)
        z = np.zeros((2, 64, 16, 2, 16), c.dtype)
        for g in range(2):
            z[g, :, :, g, :] = c[:, g].transpose(2, 0, 1)
        cc.append(z.reshape(128, 512))
    o["s5c"] = np.concatenate(cc, axis=1)
    o["consts"] = _constants()
    o["x"] = x["x"].reshape(2, 128, 1024).transpose(1, 0, 2)
    for n in ("ffn1", "ffn2"):
        o[n + "_w13"] = ffn(x[n + "_w1"][0], x[n + "_w3"][0])
        o[n + "_w2"] = rows(x[n + "_w2"][0], 2)
    w = x["w_in"][0]
    o["w_hq"], o["w_hf"] = cols(w[:, 1536:2048], 256), cols(w[:, 2048:2560], 256)
    o["w_tok"] = np.stack([rows(w[:, s:s + 512], 4) for s in (0, 512, 1024, 2560, 3072)])
    o["w_out"] = rows(x["w_out"][0], 2)
    o["ab_in"] = cols(x["ab_w_in_2"][0], 256)
    o["pool_w"] = x["pool_w_2"][0].transpose(1, 0, 2).reshape(128, 512)
    o["w_glu"] = rows(x["s5_w_glu_2"][0], 4)[0]
    o["ab_out"] = rows(x["ab_w_out_2"][0], 2)
    w = x["sb_w_qkv_2"][0]
    o["sb_q"], o["sb_k"] = cols(w[:, 0:1024], 256), cols(w[:, 1024:2048], 256)
    o["sb_v"] = np.stack([rows(w[:, s:s + 512], 4) for s in (2048, 2560)])
    o["sb_out"] = rows(x["sb_w_out_2"][0], 2)
    o["ln_g"] = np.stack([x["ln_mix_g_2"], x["ln_ffn_g_2"]], axis=1).reshape(4, 1024)
    o["ln_b"] = np.stack([x["ln_mix_b_2"], x["ln_ffn_b_2"]], axis=1).reshape(4, 1024)
    o["p"] = x["p_2"].reshape(2, 256, 2, 128).transpose(0, 3, 2, 1).reshape(2, 128, 512)
    o["ple_proj"] = np.stack([rows(x["ple_w_proj_2"][i], 2) for i in range(2)])
    o["ple_gate"] = np.stack([rows(x["ple_w_gate_2"][i], 2) for i in range(2)])
    o["moe_w13"] = np.stack([np.concatenate([ffn(x["moe_w1_2"][i, e], x["moe_w3_2"][i, e]) for e in range(16)])
                             for i in range(2)])
    o["moe_w2"] = np.stack([np.concatenate([rows(x["moe_w2_2"][i, e], 2) for e in range(16)]) for i in range(2)])
    return {k: np.ascontiguousarray(v) for k, v in o.items()}


def kernel(**inputs):
    import concourse.bacc as _bacc
    from concourse.bass_utils import run_bass_kernel_spmd as _run

    nc = _bacc.Bacc("TRN2", target_bir_lowering=False, num_devices=1)
    arrays, args = {}, {}
    for name, v in _layout(inputs).items():
        arrays[f"in_{name}"] = v
        args[name] = nc.dram_tensor(f"in_{name}", v.shape, mybir.dt.from_np(v.dtype), kind="ExternalInput").ap()
    args["out"] = nc.dram_tensor("out_0", (2, 128, 1024), F32, kind="ExternalOutput").ap().rearrange("t p d -> p t d")
    build(nc, args)
    r = _run(nc, [arrays], core_ids=[0])
    return r.results[0]["out_0"].reshape(1, 256, 1024)
```
